# Optimizing a Trainium2 kernel written in Bass

```python
import jax
import jax.numpy as jnp
from jax import lax
import numpy as np

D_MODEL = 1024
BATCH = 1
SEQ = 256
DEPTH = 1

GRID_W = 64
CTX_LEN = 256
N_MIXERS = 2
EPS = 1e-6

GLA_HEADS = 4
GLA_KDIM = D_MODEL // 2
GLA_VDIM = D_MODEL
GLA_KHEAD = GLA_KDIM // GLA_HEADS
GLA_VHEAD = GLA_VDIM // GLA_HEADS
GLA_GATE_RANK = 16
GLA_GATE_NORM = 16.0
GLA_CHUNK = 64

POOL_WINDOWS = (2, 4, 8, 16)
POOL_GROUP = D_MODEL // len(POOL_WINDOWS)

N_EXPERTS = 16
N_EXPERT_GROUPS = 4
EXPERTS_PER_GROUP = N_EXPERTS // N_EXPERT_GROUPS
TOP_K = 2
D_EXPERT = D_MODEL // 2


def _rmsnorm(x, g):
    xf = x.astype(jnp.float32)
    y = xf * lax.rsqrt(jnp.mean(xf * xf, axis=-1, keepdims=True) + EPS)
    return (y * g.astype(jnp.float32)).astype(x.dtype)

def _modulate(h, shift, scale):
    return h * (1 + scale) + shift

def _gla_scan(q, k, v, g, s0, with_outputs):
    bsz, nh, t, _ = q.shape
    dv = v.shape[-1]
    n = t // GLA_CHUNK

    def chunks(a):
        a = a.astype(jnp.float32).reshape(bsz, nh, n, GLA_CHUNK, a.shape[-1])
        return jnp.moveaxis(a, 2, 0)

    lower = jnp.tril(jnp.ones((GLA_CHUNK, GLA_CHUNK), dtype=bool))[:, :, None]

    def step(s, inp):
        qc, kc, vc, gc = inp
        cum = jnp.cumsum(gc, axis=2)
        last = cum[:, :, -1:, :]
        s_new = jnp.exp(last[:, :, 0, :])[..., None] * s + jnp.einsum(
            'bhjd,bhje->bhde', kc * jnp.exp(last - cum), vc)
        if not with_outputs:
            return s_new, None
        diff = cum[:, :, :, None, :] - cum[:, :, None, :, :]
        decay = jnp.exp(jnp.where(lower, diff, -jnp.inf))
        scores = jnp.einsum('bhid,bhjd,bhijd->bhij', qc, kc, decay)
        o = jnp.einsum('bhid,bhde->bhie', qc * jnp.exp(cum), s) + jnp.einsum(
            'bhij,bhje->bhie', scores, vc)
        return s_new, o

    s_fin, o = lax.scan(step, s0, (chunks(q), chunks(k), chunks(v), chunks(g)))
    if not with_outputs:
        return None, s_fin
    o = jnp.moveaxis(o, 0, 2).reshape(bsz, nh, t, dv)
    return o, s_fin

def _gla_project(h, w_in, w_ga, w_gb, b_g):
    bsz, t, _ = h.shape
    proj = h @ w_in
    q, k, v, r = jnp.split(proj, [GLA_KDIM, 2 * GLA_KDIM, 2 * GLA_KDIM + GLA_VDIM], axis=-1)

    def heads(a, d):
        return a.reshape(bsz, t, GLA_HEADS, d).transpose(0, 2, 1, 3)

    q = heads(q, GLA_KHEAD) * (GLA_KHEAD ** -0.5)
    k = heads(k, GLA_KHEAD)
    v = heads(v, GLA_VHEAD)
    low = jnp.einsum('btd,zdr->zbtr', h, w_ga)
    z = jnp.einsum('zbtr,zrk->zbtk', low, w_gb) + b_g[:, None, None, :]
    logdecay = jax.nn.log_sigmoid(z.astype(jnp.float32)) / GLA_GATE_NORM
    logdecay = logdecay.reshape(2, bsz, t, GLA_HEADS, GLA_KHEAD).transpose(0, 1, 3, 2, 4)
    return q, k, v, r, logdecay

def _gla_readout(o, r, norm_g, w_out):
    bsz, _, t, _ = o.shape
    o = o * lax.rsqrt(jnp.mean(o * o, axis=-1, keepdims=True) + EPS) * norm_g.astype(jnp.float32)
    o = o.transpose(0, 2, 1, 3).reshape(bsz, t, GLA_VDIM).astype(r.dtype)
    return (o * jax.nn.silu(r)) @ w_out

def _gla_mixer(h_lat, h_ctx, w_in, w_ga, w_gb, b_g, norm_g, w_out, ctx_out):
    ql, kl, vl, rl, gl = _gla_project(h_lat, w_in, w_ga, w_gb, b_g)
    qc, kc, vc, rc, gc = _gla_project(h_ctx, w_in, w_ga, w_gb, b_g)

    def flip(a):
        return jnp.flip(a, axis=2)

    s0 = jnp.zeros((h_lat.shape[0], GLA_HEADS, GLA_KHEAD, GLA_VHEAD), jnp.float32)
    oc_f, sc_f = _gla_scan(qc, kc, vc, gc[0], s0, ctx_out)
    oc_b, sc_b = _gla_scan(flip(qc), flip(kc), flip(vc), flip(gc[1]), s0, ctx_out)
    ol_f, _ = _gla_scan(ql, kl, vl, gl[0], sc_f, True)
    ol_b, _ = _gla_scan(flip(ql), flip(kl), flip(vl), flip(gl[1]), sc_b, True)
    y_lat = _gla_readout(ol_f + flip(ol_b), rl, norm_g, w_out)
    y_ctx = _gla_readout(oc_f + flip(oc_b), rc, norm_g, w_out) if ctx_out else None
    return y_lat, y_ctx

def _pool_mixer(h, w_pool, b_pool, scale):
    s, l, _ = h.shape
    hf = h.astype(jnp.float32).reshape(s, l, len(POOL_WINDOWS), POOL_GROUP)
    csum = jnp.concatenate([jnp.zeros_like(hf[:, :1]), jnp.cumsum(hf, axis=1)], axis=1)
    pos = np.arange(l)
    outs = []
    for gi, w in enumerate(POOL_WINDOWS):
        lo = np.clip(pos - w // 2, 0, l)
        hi = np.clip(pos - w // 2 + w, 0, l)
        cnt = (hi - lo).astype(np.float32)
        mean = (csum[:, hi, gi] - csum[:, lo, gi]) / cnt[None, :, None]
        outs.append(mean - hf[:, :, gi])
    pooled = jnp.stack(outs, axis=2).astype(h.dtype)
    y = jnp.einsum('slgc,gce->slge', pooled, w_pool) + b_pool
    return y.reshape(s, l, D_MODEL) * scale

def _moe(h, w_router, b_router, w1, w3, w2):
    n = h.shape[0]
    scores = jax.nn.sigmoid((h @ w_router).astype(jnp.float32))
    sel = scores + b_router.astype(jnp.float32)
    grp = sel.reshape(n, N_EXPERT_GROUPS, EXPERTS_PER_GROUP)
    grp_score = jnp.sum(lax.top_k(grp, TOP_K)[0], axis=-1)
    best = jnp.argmax(grp_score, axis=-1)
    in_group = (jnp.arange(N_EXPERTS) // EXPERTS_PER_GROUP)[None, :] == best[:, None]
    _, idx = lax.top_k(jnp.where(in_group, sel, -jnp.inf), TOP_K)
    wts = jnp.take_along_axis(scores, idx, axis=-1)
    wts = wts / jnp.sum(wts, axis=-1, keepdims=True)
    gates = jnp.sum(jax.nn.one_hot(idx, N_EXPERTS, dtype=jnp.float32) * wts[..., None], axis=1)
    gates = gates.astype(h.dtype)
    out = jnp.zeros_like(h)
    for e in range(N_EXPERTS):
        he = jax.nn.silu(h @ w1[e]) * (h @ w3[e])
        out = out + gates[:, e:e + 1] * (he @ w2[e])
    return out

def first_inputs(seed: int = 0) -> dict:
    key = jax.random.key(seed)
    ks = jax.random.split(key, 24)
    n_gla = len(range(0, DEPTH, N_MIXERS))
    n_pool = len(range(1, DEPTH, N_MIXERS))
    f32 = jnp.float32

    def nrm(k, shape, fan):
        return jax.random.normal(k, shape, f32) * (fan ** -0.5)

    def rnd(k, shape, s):
        return jax.random.normal(k, shape, f32) * s

    return {
        'x': rnd(ks[0], (BATCH, SEQ, D_MODEL), 1.0),
        'c': rnd(ks[1], (BATCH, D_MODEL), 1.0),
        'ctx': rnd(ks[2], (BATCH, CTX_LEN, D_MODEL), 1.0),
        'c_ctx': rnd(ks[3], (D_MODEL,), 1.0),
        'norm1_g': 1.0 + rnd(ks[4], (DEPTH, D_MODEL), 0.02),
        'norm2_g': 1.0 + rnd(ks[5], (DEPTH, D_MODEL), 0.02),
        'w_mod': 0.5 * nrm(ks[6], (DEPTH, D_MODEL, 6 * D_MODEL), D_MODEL),
        'b_mod': rnd(ks[7], (DEPTH, 6 * D_MODEL), 0.02),
        'gla_w_in': nrm(ks[8], (n_gla, D_MODEL, 2 * GLA_KDIM + 2 * GLA_VDIM), D_MODEL),
        'gla_w_gate_a': nrm(ks[9], (n_gla, 2, D_MODEL, GLA_GATE_RANK), D_MODEL),
        'gla_w_gate_b': nrm(ks[10], (n_gla, 2, GLA_GATE_RANK, GLA_KDIM), GLA_GATE_RANK),
        'gla_b_gate': rnd(ks[11], (n_gla, 2, GLA_KDIM), 0.1),
        'gla_norm_g': 1.0 + rnd(ks[12], (n_gla, GLA_VHEAD), 0.02),
        'gla_w_out': nrm(ks[13], (n_gla, GLA_VDIM, D_MODEL), GLA_VDIM),
        'pool_w': nrm(ks[14], (n_pool, len(POOL_WINDOWS), POOL_GROUP, POOL_GROUP), POOL_GROUP),
        'pool_b': rnd(ks[15], (n_pool, len(POOL_WINDOWS), POOL_GROUP), 0.02),
        'pool_scale': 1.0 + rnd(ks[16], (n_pool, D_MODEL), 0.1),
        'w_router': nrm(ks[17], (D_MODEL, N_EXPERTS), D_MODEL),
        'b_router': rnd(ks[18], (N_EXPERTS,), 0.01),
        'w_gate_e': nrm(ks[19], (DEPTH, N_EXPERTS, D_MODEL, D_EXPERT), D_MODEL),
        'w_up_e': nrm(ks[20], (DEPTH, N_EXPERTS, D_MODEL, D_EXPERT), D_MODEL),
        'w_down_e': nrm(ks[21], (DEPTH, N_EXPERTS, D_EXPERT, D_MODEL), D_EXPERT),
        'final_g': 1.0 + rnd(ks[22], (D_MODEL,), 0.02),
    }

def first_block(x, c, ctx, c_ctx, norm1_g, norm2_g, w_mod, b_mod, gla_w_in, gla_w_gate_a,
              gla_w_gate_b, gla_b_gate, gla_norm_g, gla_w_out, pool_w, pool_b, pool_scale,
              w_router, b_router, w_gate_e, w_up_e, w_down_e, final_g):
    bsz, t, _ = x.shape
    rows = t // GRID_W
    n_lat = bsz * t
    for i in range(DEPTH):
        mixer = i % N_MIXERS
        slot = i // N_MIXERS
        ctx_next = any(j % N_MIXERS == 0 for j in range(i + 1, DEPTH))
        use_ctx = mixer == 0 or ctx_next

        mod = jax.nn.silu(c) @ w_mod[i] + b_mod[i]
        sh1, sc1, g1, sh2, sc2, g2 = jnp.split(mod[:, None, :], 6, axis=-1)
        h = _modulate(_rmsnorm(x, norm1_g[i]), sh1, sc1)
        if use_ctx:
            mod_c = jax.nn.silu(c_ctx) @ w_mod[i] + b_mod[i]
            csh1, csc1, cg1, csh2, csc2, cg2 = jnp.split(mod_c, 6, axis=-1)
            hc = _modulate(_rmsnorm(ctx, norm1_g[i]), csh1, csc1)

        if mixer == 0:
            y, yc = _gla_mixer(h, hc, gla_w_in[slot], gla_w_gate_a[slot], gla_w_gate_b[slot],
                               gla_b_gate[slot], gla_norm_g[slot], gla_w_out[slot], ctx_next)
        else:
            y = _pool_mixer(h.reshape(bsz * rows, GRID_W, D_MODEL), pool_w[slot], pool_b[slot],
                            pool_scale[slot]).reshape(bsz, t, D_MODEL)
            yc = _pool_mixer(hc, pool_w[slot], pool_b[slot], pool_scale[slot]) if ctx_next else None

        x = x + g1 * y
        h2 = _modulate(_rmsnorm(x, norm2_g[i]), sh2, sc2).reshape(n_lat, D_MODEL)
        if ctx_next:
            ctx = ctx + cg1 * yc
            h2c = _modulate(_rmsnorm(ctx, norm2_g[i]), csh2, csc2).reshape(-1, D_MODEL)
            f = _moe(jnp.concatenate([h2, h2c], axis=0), w_router, b_router,
                     w_gate_e[i], w_up_e[i], w_down_e[i])
            x = x + g2 * f[:n_lat].reshape(bsz, t, D_MODEL)
            ctx = ctx + cg2 * f[n_lat:].reshape(ctx.shape)
        else:
            f = _moe(h2, w_router, b_router, w_gate_e[i], w_up_e[i], w_down_e[i])
            x = x + g2 * f.reshape(bsz, t, D_MODEL)
    return _rmsnorm(x, final_g)


DEPTH_2 = 2

Q_BLOCK = 128
WINDOW = 128
ROPE_BASE = 10000.0
NEG_INF = -1e30

MLA_HEADS = 8
MLA_NOPE = 64
MLA_ROPE = 32
MLA_V = 64
MLA_Q_RANK = 256
MLA_KV_RANK = 256

GQA_HEADS = 8
GQA_KV_HEADS = 2
GQA_DIM = 64

WIN_HEADS = 8
WIN_KV_HEADS = 2
WIN_DIM = 64

CONV_CH = 512
CONV_K = 3

AB_MIX = MLA_HEADS * MLA_V + GQA_HEADS * GQA_DIM
AB_SPLIT = (MLA_Q_RANK, MLA_KV_RANK, MLA_ROPE,
            GQA_HEADS * GQA_DIM, GQA_KV_HEADS * GQA_DIM, GQA_KV_HEADS * GQA_DIM,
            AB_MIX)
AB_IN = sum(AB_SPLIT)
CD_MIX = WIN_HEADS * WIN_DIM + CONV_CH
CD_SPLIT = (WIN_HEADS * WIN_DIM, WIN_KV_HEADS * WIN_DIM, WIN_KV_HEADS * WIN_DIM,
            CONV_CH, CONV_CH, CONV_CH, CD_MIX)
CD_IN = sum(CD_SPLIT)


def rmsnorm(x, gain=None):
    xf = x.astype(jnp.float32)
    y = xf * lax.rsqrt(jnp.mean(xf * xf, axis=-1, keepdims=True) + EPS)
    if gain is not None:
        y = y * gain.astype(jnp.float32)
    return y.astype(x.dtype)

def adaln(x, mod):
    shift, scale, gate = jnp.split(mod, 3, axis=-1)
    return rmsnorm(x) * (1.0 + scale) + shift, gate

def split_cols(t, sizes):
    out, off = [], 0
    for n in sizes:
        out.append(t[..., off:off + n])
        off += n
    return out

def grid_positions(n):
    rows = n // GRID_W
    row = jnp.repeat(jnp.arange(rows, dtype=jnp.float32), GRID_W)
    col = jnp.tile(jnp.arange(GRID_W, dtype=jnp.float32), rows)
    return row, col

def rope_1d(x, pos):
    half = x.shape[-1] // 2
    inv = ROPE_BASE ** (-jnp.arange(half, dtype=jnp.float32) / half)
    ang = pos[:, None] * inv[None, :]
    cos = jnp.cos(ang)[:, None, :].astype(x.dtype)
    sin = jnp.sin(ang)[:, None, :].astype(x.dtype)
    x1, x2 = x[..., :half], x[..., half:]
    return jnp.concatenate([x1 * cos - x2 * sin, x2 * cos + x1 * sin], axis=-1)

def axial_rope(x, row, col):
    half = x.shape[-1] // 2
    return jnp.concatenate([rope_1d(x[..., :half], row), rope_1d(x[..., half:], col)], axis=-1)

def rope_tail(x, rot_dim, row, col):
    return jnp.concatenate([x[..., :-rot_dim], axial_rope(x[..., -rot_dim:], row, col)], axis=-1)

def ctx_attention(q, k, v, sink=None):
    b, l, h, d = q.shape
    hk = k.shape[2]
    g = h // hk
    qg = q.reshape(b, l, hk, g, d)
    s = jnp.einsum('bqkgd,bnkd->bkgqn', qg, k, preferred_element_type=jnp.float32) * (d ** -0.5)
    if sink is not None:
        sk = jnp.broadcast_to(sink.reshape(hk, g).astype(jnp.float32)[None, :, :, None, None], (b, hk, g, l, 1))
        p = jax.nn.softmax(jnp.concatenate([s, sk], axis=-1), axis=-1)[..., :l]
    else:
        p = jax.nn.softmax(s, axis=-1)
    o = jnp.einsum('bkgqn,bnkd->bqkgd', p.astype(v.dtype), v)
    return o.reshape(b, l, h, v.shape[-1])

def joint_dense_attention(q, k, v, kc, vc):
    b, s, h, d = q.shape
    hk = k.shape[2]
    g = h // hk
    nb = s // Q_BLOCK
    kk = jnp.concatenate([kc, k], axis=1)
    vv = jnp.concatenate([vc, v], axis=1)
    qb = jnp.moveaxis(q.reshape(b, nb, Q_BLOCK, hk, g, d), 1, 0)

    def block(qi):
        sc = jnp.einsum('bqkgd,bnkd->bkgqn', qi, kk, preferred_element_type=jnp.float32) * (d ** -0.5)
        p = jax.nn.softmax(sc, axis=-1)
        return jnp.einsum('bkgqn,bnkd->bqkgd', p.astype(vv.dtype), vv)

    o = lax.map(block, qb)
    return jnp.moveaxis(o, 0, 1).reshape(b, s, h, v.shape[-1])

def joint_window_attention(q, k, v, kc, vc, sink):
    b, s, h, d = q.shape
    hk = k.shape[2]
    g = h // hk
    nb = s // Q_BLOCK
    l = kc.shape[1]
    pad = ((0, 0), (Q_BLOCK, Q_BLOCK), (0, 0), (0, 0))
    kp, vp = jnp.pad(k, pad), jnp.pad(v, pad)

    def bands(t):
        return jnp.concatenate(
            [t[:, j * Q_BLOCK: j * Q_BLOCK + s].reshape(b, nb, Q_BLOCK, hk, t.shape[-1]) for j in range(3)], axis=2)

    kb = jnp.moveaxis(bands(kp), 1, 0)
    vb = jnp.moveaxis(bands(vp), 1, 0)
    qb = jnp.moveaxis(q.reshape(b, nb, Q_BLOCK, hk, g, d), 1, 0)
    blk = jnp.arange(nb)[:, None, None] * Q_BLOCK
    qpos = blk + jnp.arange(Q_BLOCK)[None, :, None]
    kpos = blk - Q_BLOCK + jnp.arange(3 * Q_BLOCK)[None, None, :]
    mask = (jnp.abs(qpos - kpos) <= WINDOW) & (kpos >= 0) & (kpos < s)
    sink_l = sink.reshape(hk, g).astype(jnp.float32)
    scale = d ** -0.5

    def block(args):
        qi, ki, vi, mi = args
        s_loc = jnp.einsum('bqkgd,bmkd->bkgqm', qi, ki, preferred_element_type=jnp.float32) * scale
        s_loc = jnp.where(mi[None, None, None], s_loc, NEG_INF)
        s_ctx = jnp.einsum('bqkgd,blkd->bkgql', qi, kc, preferred_element_type=jnp.float32) * scale
        s_snk = jnp.broadcast_to(sink_l[None, :, :, None, None], (b, hk, g, Q_BLOCK, 1))
        p = jax.nn.softmax(jnp.concatenate([s_ctx, s_loc, s_snk], axis=-1), axis=-1)
        return (jnp.einsum('bkgql,blkd->bqkgd', p[..., :l].astype(vc.dtype), vc)
                + jnp.einsum('bkgqm,bmkd->bqkgd', p[..., l:l + 3 * Q_BLOCK].astype(vi.dtype), vi))

    o = lax.map(block, (qb, kb, vb, mask))
    return jnp.moveaxis(o, 0, 1).reshape(b, s, h, v.shape[-1])

def short_conv(u, w):
    ch = u.shape[-1]
    return lax.conv_general_dilated(u, w[:, None, :].astype(u.dtype), window_strides=(1,),
                                    padding=((CONV_K // 2, CONV_K // 2),),
                                    dimension_numbers=('NWC', 'WIO', 'NWC'), feature_group_count=ch)

def heads_ab(pp, cq_gain, ckv_gain, w_uq, w_ukv, q_gain, k_gain, qg_gain, kg_gain):
    cq, ckv, kr, gq, gk, gv, gate = split_cols(pp, AB_SPLIT)
    lead = pp.shape[:-1]
    qa = (rmsnorm(cq, cq_gain) @ w_uq).reshape(lead + (MLA_HEADS, MLA_NOPE + MLA_ROPE))
    kv = (rmsnorm(ckv, ckv_gain) @ w_ukv).reshape(lead + (MLA_HEADS, MLA_NOPE + MLA_V))
    kr_h = jnp.broadcast_to(kr[..., None, :], lead + (MLA_HEADS, MLA_ROPE))
    ka = jnp.concatenate([kv[..., :MLA_NOPE], kr_h], axis=-1)
    va = kv[..., MLA_NOPE:]
    qb = rmsnorm(gq.reshape(lead + (GQA_HEADS, GQA_DIM)), qg_gain)
    kb = rmsnorm(gk.reshape(lead + (GQA_KV_HEADS, GQA_DIM)), kg_gain)
    vb = gv.reshape(lead + (GQA_KV_HEADS, GQA_DIM))
    return rmsnorm(qa, q_gain), rmsnorm(ka, k_gain), va, qb, kb, vb, gate

def ab_layer(x, xc, mod, mod_c, w_in, w_out, cq_gain, ckv_gain, w_uq, w_ukv, q_gain, k_gain,
             qg_gain, kg_gain, row, col, update_ctx):
    b, s, _ = x.shape
    h, gate = adaln(x, mod)
    hc, gate_c = adaln(xc, mod_c)
    wts = (cq_gain, ckv_gain, w_uq, w_ukv, q_gain, k_gain, qg_gain, kg_gain)
    qa, ka, va, qb, kb, vb, g = heads_ab(h @ w_in, *wts)
    qac, kac, vac, qbc, kbc, vbc, gc = heads_ab(hc @ w_in, *wts)
    qa, ka = rope_tail(qa, MLA_ROPE, row, col), rope_tail(ka, MLA_ROPE, row, col)
    qb, kb = axial_rope(qb, row, col), axial_rope(kb, row, col)
    oa = joint_dense_attention(qa, ka, va, kac, vac).reshape(b, s, -1)
    ob = joint_dense_attention(qb, kb, vb, kbc, vbc).reshape(b, s, -1)
    mix = jnp.concatenate([oa, ob], axis=-1) * jax.nn.silu(g)
    x = x + gate * (mix @ w_out)
    if update_ctx:
        l = xc.shape[1]
        oac = ctx_attention(qac, kac, vac).reshape(b, l, -1)
        obc = ctx_attention(qbc, kbc, vbc).reshape(b, l, -1)
        mixc = jnp.concatenate([oac, obc], axis=-1) * jax.nn.silu(gc)
        xc = xc + gate_c * (mixc @ w_out)
    return x, xc

def heads_cd(pp, q_gain, k_gain):
    pq, pk, pv, gb, gcc, gh, gate = split_cols(pp, CD_SPLIT)
    lead = pp.shape[:-1]
    q = rmsnorm(pq.reshape(lead + (WIN_HEADS, WIN_DIM)), q_gain)
    k = rmsnorm(pk.reshape(lead + (WIN_KV_HEADS, WIN_DIM)), k_gain)
    v = pv.reshape(lead + (WIN_KV_HEADS, WIN_DIM))
    return q, k, v, gb, gcc, gh, gate

def cd_layer(x, xc, mod, mod_c, w_in, w_out, q_gain, k_gain, sink, conv_w, row, col, update_ctx):
    b, s, _ = x.shape
    h, gate = adaln(x, mod)
    hc, gate_c = adaln(xc, mod_c)
    q, k, v, gb, gcv, gh, g = heads_cd(h @ w_in, q_gain, k_gain)
    qc, kc, vc, gbc, gcvc, ghc, gc = heads_cd(hc @ w_in, q_gain, k_gain)
    q, k = axial_rope(q, row, col), axial_rope(k, row, col)
    oc = joint_window_attention(q, k, v, kc, vc, sink).reshape(b, s, -1)
    od = gb * short_conv(gcv * gh, conv_w)
    mix = jnp.concatenate([oc, od], axis=-1) * jax.nn.silu(g)
    x = x + gate * (mix @ w_out)
    if update_ctx:
        l = xc.shape[1]
        occ = ctx_attention(qc, kc, vc, sink).reshape(b, l, -1)
        odc = gbc * short_conv(gcvc * ghc, conv_w)
        mixc = jnp.concatenate([occ, odc], axis=-1) * jax.nn.silu(gc)
        xc = xc + gate_c * (mixc @ w_out)
    return x, xc

def second_inputs(seed: int = 0) -> dict:
    key = jax.random.key(seed)
    ks = iter(jax.random.split(key, 32))
    f32 = jnp.float32
    n_ab = (DEPTH_2 + 1) // 2
    n_cd = DEPTH_2 // 2

    def nrm(shape, scale):
        return jax.random.normal(next(ks), shape, f32) * scale

    def gain(shape):
        return 1.0 + 0.1 * jax.random.normal(next(ks), shape, f32)

    return {
        'x': nrm((BATCH, SEQ, D_MODEL), 1.0),
        'c': nrm((BATCH, D_MODEL), 1.0),
        'ctx': nrm((BATCH, CTX_LEN, D_MODEL), 1.0),
        'c_ctx': nrm((D_MODEL,), 1.0),
        'mod_w': nrm((DEPTH_2, D_MODEL, 3 * D_MODEL), D_MODEL ** -0.5),
        'mod_b': nrm((DEPTH_2, 3 * D_MODEL), 0.02),
        'ab_w_in': nrm((n_ab, D_MODEL, AB_IN), D_MODEL ** -0.5),
        'ab_w_out': nrm((n_ab, AB_MIX, D_MODEL), AB_MIX ** -0.5),
        'mla_cq_gain': gain((n_ab, MLA_Q_RANK)),
        'mla_ckv_gain': gain((n_ab, MLA_KV_RANK)),
        'mla_w_uq': nrm((n_ab, MLA_Q_RANK, MLA_HEADS * (MLA_NOPE + MLA_ROPE)), MLA_Q_RANK ** -0.5),
        'mla_w_ukv': nrm((n_ab, MLA_KV_RANK, MLA_HEADS * (MLA_NOPE + MLA_V)), MLA_KV_RANK ** -0.5),
        'mla_q_gain': gain((n_ab, MLA_NOPE + MLA_ROPE)),
        'mla_k_gain': gain((n_ab, MLA_NOPE + MLA_ROPE)),
        'gqa_q_gain': gain((n_ab, GQA_DIM)),
        'gqa_k_gain': gain((n_ab, GQA_DIM)),
        'cd_w_in': nrm((n_cd, D_MODEL, CD_IN), D_MODEL ** -0.5),
        'cd_w_out': nrm((n_cd, CD_MIX, D_MODEL), CD_MIX ** -0.5),
        'win_q_gain': gain((n_cd, WIN_DIM)),
        'win_k_gain': gain((n_cd, WIN_DIM)),
        'win_sink': nrm((n_cd, WIN_HEADS), 0.5),
        'conv_w': nrm((n_cd, CONV_K, CONV_CH), CONV_K ** -0.5),
    }

def second_block(x, c, ctx, c_ctx, mod_w, mod_b, ab_w_in, ab_w_out, mla_cq_gain, mla_ckv_gain,
              mla_w_uq, mla_w_ukv, mla_q_gain, mla_k_gain, gqa_q_gain, gqa_k_gain,
              cd_w_in, cd_w_out, win_q_gain, win_k_gain, win_sink, conv_w):
    n = x.shape[1]
    row, col = grid_positions(n)
    sc = jax.nn.silu(c)
    scc = jax.nn.silu(c_ctx)
    xc = ctx
    for i in range(DEPTH_2):
        mod = (sc @ mod_w[i] + mod_b[i])[:, None, :]
        mod_c = scc @ mod_w[i] + mod_b[i]
        j = i // 2
        update = i < DEPTH_2 - 1
        if i % 2 == 0:
            x, xc = ab_layer(x, xc, mod, mod_c, ab_w_in[j], ab_w_out[j], mla_cq_gain[j], mla_ckv_gain[j],
                             mla_w_uq[j], mla_w_ukv[j], mla_q_gain[j], mla_k_gain[j],
                             gqa_q_gain[j], gqa_k_gain[j], row, col, update)
        else:
            x, xc = cd_layer(x, xc, mod, mod_c, cd_w_in[j], cd_w_out[j], win_q_gain[j], win_k_gain[j],
                             win_sink[j], conv_w[j], row, col, update)
    return x


def setup_inputs(seed=0):
    out = dict(first_inputs(seed))
    for name, value in second_inputs(seed + 1).items():
        if name != "x":
            out[name + "_2"] = value
    return out


def reference(
    x, c, ctx, c_ctx, norm1_g, norm2_g, w_mod, b_mod, gla_w_in, gla_w_gate_a, gla_w_gate_b,
    gla_b_gate, gla_norm_g, gla_w_out, pool_w, pool_b, pool_scale, w_router, b_router, w_gate_e,
    w_up_e, w_down_e, final_g, c_2, ctx_2, c_ctx_2, mod_w_2, mod_b_2, ab_w_in_2, ab_w_out_2,
    mla_cq_gain_2, mla_ckv_gain_2, mla_w_uq_2, mla_w_ukv_2, mla_q_gain_2, mla_k_gain_2,
    gqa_q_gain_2, gqa_k_gain_2, cd_w_in_2, cd_w_out_2, win_q_gain_2, win_k_gain_2, win_sink_2,
    conv_w_2,
):
    x = first_block(
        x, c, ctx, c_ctx, norm1_g, norm2_g, w_mod, b_mod, gla_w_in, gla_w_gate_a, gla_w_gate_b,
        gla_b_gate, gla_norm_g, gla_w_out, pool_w, pool_b, pool_scale, w_router, b_router,
        w_gate_e, w_up_e, w_down_e, final_g,
    )
    return second_block(
        x, c_2, ctx_2, c_ctx_2, mod_w_2, mod_b_2, ab_w_in_2, ab_w_out_2, mla_cq_gain_2,
        mla_ckv_gain_2, mla_w_uq_2, mla_w_ukv_2, mla_q_gain_2, mla_k_gain_2, gqa_q_gain_2,
        gqa_k_gain_2, cd_w_in_2, cd_w_out_2, win_q_gain_2, win_k_gain_2, win_sink_2, conv_w_2,
    )


_drawn_inputs = setup_inputs


def setup_inputs(seed=0):
    import zlib

    import numpy as np

    out = dict(_drawn_inputs(seed))
    spreads = {}
    factors = {'gla_norm_g': 3.41,
     'mla_cq_gain_2': 8.0,
     'mla_ckv_gain_2': 2.946,
     'mla_q_gain_2': 8.0,
     'mla_k_gain_2': 8.0,
     'gqa_q_gain_2': 8.0,
     'gqa_k_gain_2': 8.0,
     'win_q_gain_2': 8.0,
     'win_k_gain_2': 8.0,
     'win_sink_2': 8.0}
    for name, (base, spread) in spreads.items():
        noise = np.random.default_rng([zlib.crc32(name.encode()), seed]).standard_normal(out[name].shape)
        drawn = base * np.exp(spread * noise) if base else spread * noise
        out[name] = jnp.asarray(drawn.astype(out[name].dtype))
    for name, factor in factors.items():
        out[name] = (out[name] * factor).astype(out[name].dtype)
    return out
```

```python
import math
from contextlib import ExitStack

import numpy as np
import concourse.bass as bass
from concourse import mybir

F32 = mybir.dt.float32
I32 = mybir.dt.int32
U32 = mybir.dt.uint32
ALU = mybir.AluOpType
ACT = mybir.ActivationFunctionType
AX = mybir.AxisListType
LN_EXP = "natural_log_exp_and_others"

P = 128
D = 1024
KC = D // P
T = 256
TT = T // P
EPS = 1e-6

HG = 4
DK = 128
DV = 256
GATE_RANK = 16
GATE_NORM = 16.0
LEVELS = [128, 64, 32, 16, 8, 4, 2, 1]

NE = 16
GROUPS = 4
EPG = NE // GROUPS
FF = 512
CAP = 64
EXTRA = T // CAP - 1

MH, NOPE, ROT, MV = 8, 64, 32, 64
MD = NOPE + ROT
RANK = 256
GH, KVH, GD = 8, 2, 64
GPK = GH // KVH
CONV_CH, TAPS = 512, 3
ROPE_BASE, GRID_W = 10000.0, 64
NEG = -1e30

SLOT = KC * 512
SLOTS = 3
MAIN = 14336


def constant_columns():
    widths = [("ident", P), ("ones", 256), ("before", P), ("iota", T), ("levels", P * (len(LEVELS) - 1)),
              ("window", 2 * P), ("rope_mla", 2 * 2 * 16), ("rope_gqa", 2 * 2 * 32), ("sum_quadrants", 2),
              ("row_base", NE), ("earlier", EPG * EPG), ("eps", 1), ("log_q_mla", 1), ("log_q_gqa", 1)]
    at, out = 0, {}
    for name, w in widths:
        out[name] = (at, w)
        at += w
    return out, at


def constant_table():
    cols, width = constant_columns()
    c = np.zeros((P, width), np.float32)

    def put(name, a):
        s, w = cols[name]
        c[:, s:s + w] = np.asarray(a, np.float32).reshape(P, w)

    i = np.arange(P)
    put("ident", np.eye(P))
    put("ones", np.ones((P, 256)))
    put("before", i[:, None] < i[None, :])
    put("iota", np.tile(np.arange(T), (P, 1)))
    lev = []
    for b in LEVELS[1:]:
        bj, bi = i[:, None] // b, i[None, :] // b
        lev.append((bj != bi) & (bj // 2 == bi // 2))
    put("levels", np.stack(lev, 1))
    put("window", np.stack([np.where(i[None, :] <= i[:, None], 0.0, NEG),
                            np.where(i[None, :] >= i[:, None], 0.0, NEG)], 1))
    tok = np.arange(T)
    pos = np.stack([tok // GRID_W, tok % GRID_W], 1).astype(np.float32)

    def rope(half):
        inv = np.float32(ROPE_BASE) ** (-np.arange(half, dtype=np.float32) / np.float32(half))
        ang = (pos[:, :, None] * inv[None, None, :]).astype(np.float32)
        t = np.stack([np.cos(ang), np.sin(ang)], 1)
        return t.reshape(TT, P, -1).transpose(1, 0, 2)

    put("rope_mla", rope(8))
    put("rope_gqa", rope(16))
    q = np.zeros((P, 2))
    for j in range(4):
        for m in range(2):
            q[32 * j + m, m] = 1
    put("sum_quadrants", q)
    put("row_base", np.tile(np.arange(NE) * T, (P, 1)))
    e = np.arange(EPG)
    put("earlier", np.tile((e[None, :] < e[:, None]).astype(np.float32).reshape(1, -1), (P, 1)))
    put("eps", np.full(P, EPS))
    put("log_q_mla", np.full(P, -0.5 * math.log(MD)))
    put("log_q_gqa", np.full(P, -0.5 * math.log(GD)))
    return c


class Banks:

    def __init__(self, banks, full):
        self.banks, self.full, self.freed, self.at = banks, full, [], {}

    def open(self, pe, name, sem, value):
        n = len(self.freed)
        if n >= 8:
            pe.wait_ge(*self.freed[n - 8])
        self.freed.append((sem, value))
        self.at[name] = n
        return self.banks[n % 8]

    def filled(self, name, ins):
        ins.then_inc(self.full[self.at[name] % 8], 1)

    def wait(self, eng, name):
        n = self.at[name]
        eng.wait_ge(self.full[n % 8], n // 8 + 1)
        return self.banks[n % 8]


def build(nc, a, out):
    ctx = ExitStack()
    with ctx:
        def sb(name, shape, dt=F32):
            return ctx.enter_context(nc.sbuf_tensor(name, shape, dt))

        def sem(name):
            return ctx.enter_context(nc.semaphore(name))

        cols, ncon = constant_columns()
        con = sb("con", [P, ncon])

        def K(name):
            s, w = cols[name]
            return con[:, s:s + w]

        ident, ones, before = K("ident"), K("ones")[:, 0:P], K("before")
        ones256 = K("ones")
        iota = K("iota")
        level_masks = K("levels").rearrange("p (l i) -> p l i", i=P).bitcast(I32)
        window = K("window").rearrange("p (t k) -> p t k", t=2)
        rope_mla = K("rope_mla").rearrange("p (t c a f) -> p t c a f", t=TT, c=2, a=2)
        rope_gqa = K("rope_gqa").rearrange("p (t c a f) -> p t c a f", t=TT, c=2, a=2)
        sum_quadrants = K("sum_quadrants")
        row_base = K("row_base")
        earlier = K("earlier").rearrange("p (i j) -> p i j", j=EPG)
        eps, log_q_mla, log_q_gqa = K("eps"), K("log_q_mla"), K("log_q_gqa")

        gain_widths = [("gla_norm_g", DV), ("b_router", NE), ("mla_cq_gain_2", RANK), ("mla_ckv_gain_2", RANK),
                       ("mla_q_gain_2", MD), ("mla_k_gain_2", MD), ("gqa_q_gain_2", GD), ("gqa_k_gain_2", GD),
                       ("win_q_gain_2", GD), ("win_k_gain_2", GD), ("win_sink_2", GH)]
        gains = sb("gains", [P, sum(w for _, w in gain_widths)])
        gain, at = {}, 0
        for n, w in gain_widths:
            gain[n] = gains[:, at:at + w]
            at += w

        rows_sb = sb("rows_sb", [P, 2, P])
        row_list = [("c", 8, 0), ("c_ctx", 8, 0), ("c_2", 8, 0), ("c_ctx_2", 8, 0), ("norm1_g", 8, 0),
                    ("norm2_g", 8, 0), ("gla_b_gate", 8, 0), ("conv_w_2", TAPS * 4, 0),
                    ("b_mod", 48, 1), ("mod_b_2", 48, 1)]
        nrow = [0, 0]
        row_at = {}
        for n, r, half in row_list:
            row_at[n] = (nrow[half], r, half)
            nrow[half] += r
        colv = sb("colv", [P, nrow[0] + nrow[1]])

        def column(name):
            s, r, half = row_at[name]
            s += half * nrow[0]
            return colv[:, s:s + r]

        silu_c = sb("silu_c", [P, 2, KC, 32])
        mod_rows = sb("mod_rows", [P, 2, 512])
        mod1 = sb("mod1", [P, 48, 2])
        mod2 = sb("mod2", [P, 2, 24, 2])
        coef = sb("coef", [P, 7, 2, KC])
        X = sb("X", [P, 4, D])
        gate_a = sb("gate_a", [P, KC, 2, GATE_RANK])
        w_route = sb("w_route", [P, KC, NE])
        gate_rows = sb("gate_rows", [P, 2, D])
        gate_diag = sb("gate_diag", [P, KC, P])
        sums = sb("sums", [P, 48])
        rstd = sb("rstd", [P, 48])
        small = sb("small", [P, 1024 - 256 - 96])
        route_idx = sb("route_idx", [P, TT, 2], I32)
        extra_flag = sb("extra_flag", [P, NE, EXTRA], I32)

        arena = sb("arena", [P, MAIN + 6 * SLOT])
        HIGH = MAIN
        RING = MAIN + 3 * SLOT

        def view(off, *dims):
            n = int(np.prod(dims))
            v = arena[:, off:off + n]
            if len(dims) == 1:
                return v
            names = "abcde"[:len(dims)]
            return v.rearrange("p (%s) -> p %s" % (" ".join(names), " ".join(names)),
                               **{names[i]: dims[i] for i in range(len(dims))})

        def slot_at(s):
            return RING + s * SLOT if s < 3 else HIGH + (s - 3) * SLOT

        hT = view(0, KC, 512)
        qT = view(4096, HG, T)
        kT = view(5120, HG, 512)
        r_sb = view(7168, TT, D)
        xn = view(9216, 4, D)
        v_sb = view(9216, 4, D)
        low = view(13312, 2, 512)
        kd = view(0, 2, HG, TT, P)
        sc_diag = view(2048, HG * TT, P)
        sc_off = view(3072, HG, 2, P)
        zg = view(HIGH, 2, HG, 512)
        zt = view(HIGH + 8192, 2, HG, 512)
        gate_b = view(HIGH + 4096, 2, 512)
        cum = view(HIGH + 4096, 2, HG, 2, T + 1)
        lev = [view(HIGH, 2, HG, T), view(HIGH + 2048, 2, HG, T)]
        kdT = lev[0]
        S_sb = view(HIGH + 8208, 2 * HG, DV)
        qdec = [view(13312, HG, T), view(HIGH + 10256, HG, T)]
        o_sb = view(HIGH, TT, D)
        oT = view(HIGH + 2048, KC, T)
        y_t1 = view(HIGH + 11280, 512)
        hg = view(0, KC, NE * CAP)
        sel = view(8192, TT, NE * CAP)
        xn2 = view(10240, TT, D)
        h2T = view(12288, KC, T)
        hs = [view(12288, KC, CAP), view(12800, KC, CAP)]
        act1, act2 = view(13312, 256), view(13568, 256)
        ffT = view(13824, 2, P)
        sel_x = view(14080, TT, CAP)
        y_buf = [view(8192, 512), view(8704, 512)]
        y_x, hs_x = view(9216, 512), view(9728, KC, CAP)
        y_tok = view(HIGH + 4096, TT, 2, D)
        final_row = view(HIGH + 8192, D)
        mixT4 = view(0, KC, 512)
        pj = view(4096, 4, 672)
        cT = view(6784, 4, 512)
        gates4 = view(8832, 4, D)
        QT, KT = view(HIGH, MH, 512), view(HIGH + 4096, MH, 512)
        qbT = view(HIGH + 8192, 4, 512)
        VA = view(HIGH + 10240, 4, MH * MV)
        kbT = view(12928, 512)
        VB = view(13440, 4, P)
        cn = view(HIGH, 2, 512)
        SCRATCH = RING + 2 * SLOT
        q_t, k_t = ([view(SCRATCH + (2 * i + j) * MH * MD, MH, MD) for j in range(2)] for i in range(2))
        tmp1 = view(SCRATCH + 4 * MH * MD, MH * MD)
        prob = [view(4096 + 512 * i, 512) for i in range(3)]
        probT = [view(4096 + 1536 + 512 * i, 512) for i in range(3)]
        cq_sb = view(4096 + 3072, TT, 512)
        ckv_sb = view(4096 + 4096, 4, 256)
        ga_sb = view(8192 + 1024, TT, 512)
        gbT, gcT, ghT = view(10240, 4, T), view(11264, 4, T), view(12288, 4, T)
        gaT = view(13312, 4, T)
        u_pad = view(HIGH, 4, T + 2)
        conv = view(HIGH + 1032, 4, T)
        qwT = view(HIGH + 2056, 4, T)
        kwT = view(HIGH + 3080, 512)
        mixT2 = view(HIGH + 3592, KC, T)
        ctmp1, ctmp2 = view(HIGH + 5640, 512), view(HIGH + 6152, 512)

        y_rows = nc.dram_tensor("y_rows", [NE * T, D], F32, kind="Internal").ap()

        banks = Banks([ctx.enter_context(nc.psum_tensor(f"bank{i}", [P, 512], F32)) for i in range(8)],
                      [sem(f"bank{i}_full") for i in range(8)])

        def cols_of(w, c0, n):
            return w.rearrange("(k p) c -> p k c", p=P)[:, :, c0:c0 + n]

        mod_chunks = [(0, c) for c in range(12)] + [(1, c) for c in range(6)] + [(2, c) for c in range(6)]
        w_in = a["gla_w_in"][0]
        ab_in, cd_in = a["ab_w_in_2"][0], a["cd_w_in_2"][0]
        loads = []
        slot_turn = [0]

        def load(name, src, kdim, n):
            loads.append((name, src, slot_turn[0] % SLOTS, kdim, n))
            slot_turn[0] += 1

        def load_mod(m):
            l, c = mod_chunks[m]
            src = a["w_mod"][0] if l == 0 else a["mod_w_2"][l - 1]
            load(f"mod{m}", cols_of(src, 512 * c, 512), KC, 512)

        for m in range(4):
            load_mod(m)
        GLA_COLS = [("k", 512), ("q", 0), ("v0", 1024), ("v1", 1536), ("r0", 2048), ("r1", 2560)]
        for i, (n, c0) in enumerate(GLA_COLS):
            load(n, cols_of(w_in, c0, 512), KC, 512)
            load_mod(4 + i)
        for i in range(8):
            load_mod(10 + i)
        for c in range(2):
            load(f"o{c}", cols_of(a["gla_w_out"][0], 512 * c, 512), KC, 512)
        N_BEFORE = len(loads)
        AB_COLS = [("ab0", 0, 512), ("ab1", 512, 512), ("ab2", 1024, 288), ("ab3", 1312, 512), ("ab4", 1824, 512)]
        slot_turn[0] = 0
        AB_COLS, ab_gates = AB_COLS[:3], AB_COLS[3:]
        for n, c0, w in AB_COLS:
            load(n, cols_of(ab_in, c0, w), KC, w)
        slot_turn[0] = 0
        load("ab3", cols_of(ab_in, ab_gates[0][1], 512), KC, 512)
        load("uq", a["mla_w_uq_2"][0].rearrange("(k p) c -> p k c", p=P), 2, MH * MD)
        w_ukv = view(slot_at(1) + 2 * MH * MD, 2, MH * P)
        slot_turn[0] = 0
        load("ab4", cols_of(ab_in, ab_gates[1][1], 512), KC, 512)
        for m in range(18, 24):
            load_mod(m)
        for c in range(2):
            load(f"abo{c}", cols_of(a["ab_w_out_2"][0], 512 * c, 512), KC, 512)
        CD_COLS = [("cd0", 0, 512), ("cd1", 512, 256), ("cd2", 768, 512), ("cd3", 1280, 512), ("cd4", 1792, 512),
                   ("cd5", 2304, 512), ("cd6", 2816, 512)]
        for n, c0, w in CD_COLS:
            load(n, cols_of(cd_in, c0, w), KC, w)
        for c in range(2):
            load(f"cdo{c}", cols_of(a["cd_w_out_2"][0], 512 * c, 512), KC, 512)

        landed = [sem(f"slot{s}_landed") for s in range(6)]
        fills = {}
        count = [0] * 6
        for n, ld in enumerate(loads):
            if n == N_BEFORE:
                before_experts = list(count)
                for s in range(6):
                    count[s] += NE // 2
            s = ld[2]
            count[s] += 1
            fills[ld[0]] = (s, count[s])
        last_use = {}

        def weights(pe, name):
            s, c = fills[name]
            pe.wait_ge(landed[s], 16 * c)
            ld = [x for x in loads if x[0] == name][0]
            return view(slot_at(s), ld[3], ld[4])

        con_in, rows_in, gains_in, small_w_in = sem("con_in"), sem("rows_in"), sem("gains_in"), sem("small_w_in")
        pj0_ready, ga_copied, ukv_in = sem("pj0_ready"), sem("ga_copied"), sem("ukv_in")
        gate_rows_zero, rows_zeroed = sem("gate_rows_zero"), sem("rows_zeroed")
        gate_b_in, final_in = sem("gate_b_in"), sem("final_in")
        x_in, ctx_in, ctx2_in = sem("x_in"), sem("ctx_in"), sem("ctx2_in")
        out_sem = sem("out_written")
        silu_zeroed = sem("silu_zeroed")
        pad_zeroed = sem("pad_zeroed")
        a_step, v_step = sem("act_step"), sem("dve_step")
        cols_ready = sem("cols_ready")
        silu_ready = sem("silu_ready")
        row_ready = sem("mod_row_ready")
        modcol_ready = sem("mod_cols_ready")
        coef_ready = sem("coef_ready")
        rstd_ready = sem("rstd_ready")
        xn_ready = sem("xn_ready")
        turned_a, turned_v = sem("turned_by_act"), sem("turned_by_dve")
        k_ready, q_ready, low_ready = sem("k_ready"), sem("q_ready"), sem("low_ready")
        z_ready, v_ready, r_ready = sem("z_ready"), sem("v_ready"), sem("r_ready")
        softplus_ready, cum_ready = sem("softplus_ready"), sem("cum_ready")
        kd_arg, kd_exp, kd_ready, kd_turned = sem("kd_arg"), sem("kd_exp"), sem("kd_ready"), sem("kd_turned")
        qd_arg, qd_exp, qd_ready = sem("qd_arg"), sem("qd_exp"), sem("qd_ready")
        lev_arg, lev_exp, lev_ready, lev_used = sem("lev_arg"), sem("lev_exp"), sem("lev_ready"), sem("lev_used")
        state_ready, diag_ready, off_ready = sem("state_ready"), sem("diag_ready"), sem("off_ready")
        o_copied, o_rstd, o_ready, oT_ready = sem("o_copied"), sem("o_rstd"), sem("o_ready"), sem("oT_ready")
        diag_gate, gate_bc, y_added = sem("diag_gate"), sem("gate_broadcast"), sem("y_added")
        logit_exp, routed, sel_ready, ranked = sem("logit_exp"), sem("routed"), sem("sel_ready"), sem("ranked")
        hg_a, hg_v = sem("gathered_by_act"), sem("gathered_by_dve")
        hs_ready, up_done, silu_done, ff_ready = sem("hs_ready"), sem("up_done"), sem("silu_done"), sem("ff_ready")
        ff_turned, ffT_ready, down_done, ye_ready = sem("ff_turned"), sem("ffT_ready"), sem("down_done"), sem("ye_ready")
        stored = [sem("stored0"), sem("stored1")]
        x_sel, x_gath, x_h, x_up, x_silu = sem("x_sel"), sem("x_gath"), sem("x_h"), sem("x_up"), sem("x_silu")
        x_ff, x_turned, x_ffT, x_down, x_ye, x_stored = (sem("x_ff"), sem("x_turned"), sem("x_ffT"), sem("x_down"),
                                                         sem("x_ye"), sem("x_stored"))
        experts_done, gathered_y = sem("experts_done"), sem("gathered_y")
        block1_done, x_moe = sem("block1_done"), sem("x_moe")
        c_ms, c_ready, c_copied = sem("c_ms"), sem("c_ready"), sem("c_copied")
        pj_ready, gate4_ready = sem("pj_ready"), sem("gate4_ready")
        qa_copied, kv_copied, qk_rstd, qk_ms = sem("qa_copied"), sem("kv_copied"), sem("qk_rstd"), sem("qk_ms")
        qk_ready, qkT_ready = sem("qk_ready"), sem("qkT_ready")
        gqk_ready, gqkT_ready = sem("gqk_ready"), sem("gqkT_ready")
        s_max, s_exp, pT_a, pT_v, mixed = sem("s_max"), sem("s_exp"), sem("pT_by_act"), sem("pT_by_dve"), sem("mixed")
        mixT_ready = sem("mixT_ready")
        cdq_ready, cdkv_ready, cdg_ready, cdT_ready, cd_conv = (sem("cdq_ready"), sem("cdkv_ready"), sem("cdg_ready"),
                                                                sem("cdT_ready"), sem("cd_conv"))
        sink_exp = sem("sink_exp")

        block = ctx.enter_context(nc.Block())

        NORM_TILES = [range(4), range(2), range(2, 4), range(2), range(2), range(4)]
        TURN_TILES = [range(4), range(2), range(2, 4), range(2), range(4)]
        XN_BEFORE = [0, 4, 6, 8, 10]
        AB_ORDER = [2, 3, 0, 1]
        AB_AT = {t: n for n, t in enumerate(AB_ORDER)}
        AB_STEPS = [("grouped norm", 2), ("project", 0), ("grouped norm", 3), ("project", 1), ("gates", 0),
                    ("latent norm", 0), ("gates", 1)] + [("grouped", n) for n in range(4)] + \
            [("gates", 2), ("latent norm", 1), ("gates", 3), ("latent", 0), ("project", 2), ("latent", 1),
             ("project", 3), ("gates", 4), ("latent norm", 2), ("gates", 5), ("gates", 6), ("latent", 2),
             ("latent norm", 3), ("gates", 7), ("latent", 3)]
        MLA_UNITS = [(h, t) for h in range(MH) for t in range(4)]
        GQA_UNITS = [(h, t) for h in range(GH) for t in range(4)]
        AB_UNITS = [("m", h, t) for h, t in MLA_UNITS] + [("g", h, t) for h, t in GQA_UNITS]
        CD_UNITS = [("w", h, t) for h in range(GH) for t in range(TT)]
        NU = len(AB_UNITS)

        @block.tensor
        def _(pe):
            mod_pending = []

            def mod_cols(m):
                pe.wait_ge(row_ready, m + 1)
                ps = banks.open(pe, f"col{m}", modcol_ready, m + 1)
                for c in range(4):
                    mm = pe.matmul(ps[:, 2 * c:2 * c + 2], mod_rows[:, m % 2, c * P:(c + 1) * P], sum_quadrants,
                                   start=True, stop=True)
                banks.filled(f"col{m}", mm)

            def mod(m):
                w = weights(pe, f"mod{m}")
                if m == 0:
                    pe.wait_ge(silu_ready, 4)
                blk = 0 if m < 12 else 1
                ps = banks.open(pe, f"row{m}", row_ready, m + 1)
                for k in range(KC):
                    j = k % 4
                    mm = pe.matmul(ps[32 * j:32 * j + 32, :], silu_c[:, blk, k, :], w[:, k, :],
                                   start=(k < 4), stop=(k >= 4), tile_position=(0, 32 * j))
                banks.filled(f"row{m}", mm)
                last_use[f"mod{m}"] = f"row{m}"
                if mod_pending:
                    mod_cols(mod_pending.pop())
                mod_pending.append(m)

            def mod_flush():
                mod_cols(mod_pending.pop())

            def turn(use, src):
                ts = TURN_TILES[use]
                pe.wait_ge(xn_ready, XN_BEFORE[use] + len(ts))
                for k in range(KC):
                    s = (turned_a, turned_v)[k % 2]
                    ps = banks.open(pe, f"turn{use}_{k}", s, 4 * use + k // 2 + 1)
                    for t in ts:
                        mm = pe.transpose(ps[:, t * P:(t + 1) * P], src[:, t, k * P:(k + 1) * P], ident)
                    banks.filled(f"turn{use}_{k}", mm)

            def wait_turned(use):
                pe.wait_ge(turned_a, 4 * use + 4)
                pe.wait_ge(turned_v, 4 * use + 4)

            def project(name, wname, c0, n, tile, lhs, sem_, value):
                w = weights(pe, wname)
                kd_ = w.shape[1]
                ps = banks.open(pe, name, sem_, value)
                for k in range(kd_):
                    mm = pe.matmul(ps[:, 0:n], lhs[:, k, tile * P:(tile + 1) * P], w[:, k, c0:c0 + n],
                                   start=(k == 0), stop=(k == kd_ - 1))
                banks.filled(name, mm)
                last_use[wname] = name

            def project_T(name, wname, chunks, rhs_cols, rhs, sem_, value):
                w = weights(pe, wname)
                ps = banks.open(pe, name, sem_, value)
                n = rhs_cols
                for i, c in enumerate(chunks):
                    for k in range(KC):
                        mm = pe.matmul(ps[:, i * n:(i + 1) * n], w[:, k, c * P:(c + 1) * P], rhs[:, k, 0:n],
                                       start=(k == 0), stop=(k == KC - 1))
                banks.filled(name, mm)
                last_use[wname] = name

            def gate(u):
                pe.wait_ge(diag_gate, u + 1)
                for h in range(2):
                    ps = banks.open(pe, f"gate{u}_{h}", gate_bc, 2 * u + h + 1)
                    mm = pe.matmul(ps[:, :], ones, gate_diag[:, 4 * h:4 * h + 4, :], start=True, stop=True)
                    banks.filled(f"gate{u}_{h}", mm)

            pe.wait_ge(con_in, 16)
            pe.wait_ge(rows_in, 16 * len(row_list))
            for half in range(2):
                ps = banks.open(pe, f"cols{half}", cols_ready, half + 1)
                n = nrow[half]
                mm = pe.transpose(ps[:, 0:n], rows_sb[0:n, half, :], ident[0:n, 0:n])
                banks.filled(f"cols{half}", mm)
            for m in range(4):
                mod(m)
            mod_flush()

            turn(0, xn)
            wait_turned(0)
            for h in range(HG):
                project_T(f"k{h}", "k", [h], 512, hT, k_ready, h + 1)
            mod(4)
            for g in range(2):
                project_T(f"q{g}", "q", [2 * g, 2 * g + 1], T, hT, q_ready, g + 1)
            mod(5)
            pe.wait_ge(small_w_in, 16 * 3)
            for z in range(2):
                ps = banks.open(pe, f"low{z}", low_ready, z + 1)
                for k in range(KC):
                    mm = pe.matmul(ps[0:GATE_RANK, :], gate_a[:, k, z, :], hT[:, k, :],
                                   start=(k == 0), stop=(k == KC - 1))
                banks.filled(f"low{z}", mm)
            for t in range(2):
                project(f"v0_{t}", "v0", 0, 512, t, hT, v_ready, t + 1)
            pe.wait_ge(gate_b_in, 32)
            pe.wait_ge(low_ready, 2)
            for z in range(2):
                for h in range(HG):
                    n = z * HG + h
                    ps = banks.open(pe, f"z{n}", z_ready, n + 1)
                    mm = pe.matmul(ps[:, :], gate_b[0:GATE_RANK, z, h * DK:(h + 1) * DK], low[0:GATE_RANK, z, :],
                                   start=True, stop=True)
                    banks.filled(f"z{n}", mm)
            for t in range(2, 4):
                project(f"v0_{t}", "v0", 0, 512, t, hT, v_ready, t + 1)
            mod(6)
            for t in range(4):
                project(f"v1_{t}", "v1", 0, 512, t, hT, v_ready, t + 5)
            mod(7)
            for t in range(TT):
                project(f"r0_{t}", "r0", 0, 512, t, hT, r_ready, t + 1)
            mod(8)
            for t in range(TT):
                project(f"r1_{t}", "r1", 0, 512, t, hT, r_ready, t + 3)
            mod(9)

            pe.wait_ge(kd_ready, 1)
            for g in range(4):
                z, h0 = g // 2, 2 * (g % 2)
                ps = banks.open(pe, f"kd{g}", kd_turned, g + 1)
                for i in range(4):
                    h, t = h0 + i // 2, i % 2
                    mm = pe.transpose(ps[:, i * P:(i + 1) * P], kdT[:, z, h, t * P:(t + 1) * P], ident)
                banks.filled(f"kd{g}", mm)
            for g in range(2):
                ps = banks.open(pe, f"same{g}", diag_ready, g + 1)
                for i in range(4):
                    h, b = (4 * g + i) // 2, i % 2
                    mm = pe.matmul(ps[:, i * P:(i + 1) * P], kT[:, h, b * P:(b + 1) * P], qT[:, h, b * P:(b + 1) * P],
                                   start=True, stop=True)
                banks.filled(f"same{g}", mm)
            pe.wait_ge(kd_turned, 4)
            for g in range(4):
                ps = banks.open(pe, f"state{g}", state_ready, g + 1)
                for i in range(2):
                    z, h = (2 * g + i) // HG, (2 * g + i) % HG
                    for t in range(TT):
                        mm = pe.matmul(ps[:, i * DV:(i + 1) * DV], kd[:, z, h, t, :], v_sb[:, 2 + t, h * DV:(h + 1) * DV],
                                       start=(t == 0), stop=(t == TT - 1))
                banks.filled(f"state{g}", mm)

            for li, b in enumerate(LEVELS):
                pe.wait_ge(lev_ready, li + 1)
                L = lev[(li + 1) % 2]
                for g in range(2):
                    if li == 0:
                        name = f"off{g}"
                        ps = banks.open(pe, name, off_ready, g + 1)
                    else:
                        name = f"lev{li}_{g}"
                        ps = banks.open(pe, name, lev_used, 2 * (li - 1) + g + 1)
                    for i in range(4):
                        h, s = (4 * g + i) // 2, i % 2
                        jb, ib = (s, 1 - s) if li == 0 else (s, s)
                        mm = pe.matmul(ps[:, i * P:(i + 1) * P], L[:, 1, h, jb * P:(jb + 1) * P],
                                       L[:, 0, h, ib * P:(ib + 1) * P], start=True, stop=True)
                    banks.filled(name, mm)
                mod(10 + li)
            mod_flush()

            pe.wait_ge(lev_used, 14)
            pe.wait_ge(off_ready, 2)
            pe.wait_ge(qd_ready, 2)
            pe.wait_ge(state_ready, 4)
            for t in range(TT):
                for hp in range(2):
                    n = 2 * t + hp
                    ps = banks.open(pe, f"o{t}{hp}", o_copied, n + 1)
                    for i in range(2):
                        h = 2 * hp + i
                        o = ps[:, i * DV:(i + 1) * DV]
                        pe.matmul(o, sc_diag[:, TT * h + t, :], v_sb[:, t, h * DV:(h + 1) * DV], start=True, stop=False)
                        pe.matmul(o, sc_off[:, h, 1 - t, :], v_sb[:, 1 - t, h * DV:(h + 1) * DV], start=False, stop=False)
                        for z in range(2):
                            mm = pe.matmul(o, qdec[z][:, h, t * P:(t + 1) * P], S_sb[:, z * HG + h, :],
                                           start=False, stop=(z == 1))
                    banks.filled(f"o{t}{hp}", mm)
            gate(0)
            pe.wait_ge(o_ready, TT)
            for g in range(4):
                ps = banks.open(pe, f"oT{g}", oT_ready, g + 1)
                for i in range(4):
                    c, t = 2 * g + i // 2, i % 2
                    mm = pe.transpose(ps[:, i * P:(i + 1) * P], o_sb[:, t, c * P:(c + 1) * P], ident)
                banks.filled(f"oT{g}", mm)
            pe.wait_ge(oT_ready, 4)
            for c in range(2):
                for t in range(TT):
                    project(f"y{c}{t}", f"o{c}", 0, 512, t, oT, y_added, 2 * c + t + 1)

            turn(1, xn2)
            wait_turned(1)
            ps = banks.open(pe, "logits", logit_exp, 1)
            for t in range(TT):
                for k in range(KC):
                    mm = pe.matmul(ps[:, t * NE:(t + 1) * NE], h2T[:, k, t * P:(t + 1) * P], w_route[:, k, :],
                                   start=(k == 0), stop=(k == KC - 1))
            banks.filled("logits", mm)
            gate(1)
            pe.wait_ge(routed, 1)
            mask = small[:, 96:128].rearrange("p (t e) -> p t e", t=TT)
            ps = banks.open(pe, "ranks", ranked, 1)
            pe.matmul(ps[:, 0:NE], before, mask[:, 0, :], start=True, stop=True)
            pe.matmul(ps[:, NE:2 * NE], ones, mask[:, 0, :], start=True, stop=False)
            pe.matmul(ps[:, NE:2 * NE], before, mask[:, 1, :], start=False, stop=True)
            pe.matmul(ps[:, 2 * NE:3 * NE], ones, mask[:, 0, :], start=True, stop=False)
            mm = pe.matmul(ps[:, 2 * NE:3 * NE], ones, mask[:, 1, :], start=False, stop=True)
            banks.filled("ranks", mm)
            pe.wait_ge(sel_ready, TT)
            for half in range(2):
                for k in range(KC):
                    name = f"gath{half}_{k}"
                    s = (hg_a, hg_v)[k % 2]
                    ps = banks.open(pe, name, s, 4 * half + k // 2 + 1)
                    for t in range(TT):
                        mm = pe.matmul(ps[:, :], xn2[:, t, k * P:(k + 1) * P], sel[:, t, 512 * half:512 * half + 512],
                                       start=(t == 0), stop=(t == TT - 1))
                    banks.filled(name, mm)

            moe = [banks.open(pe, f"moe{i}", experts_done, 1) for i in range(4)]
            up_b, t_b, dn_b, xg_b = moe

            def up(h, s0, sem_):
                w13 = view(slot_at(s0), 2, KC, 512)
                for k in range(KC):
                    for j in range(2):
                        mm = pe.matmul(up_b[64 * j:64 * j + 64, :], h[:, k, :], w13[:, :, k, 256 * j:256 * j + 256],
                                       start=(k == 0), stop=(k == KC - 1), tile_position=(0, 64 * j))
                mm.then_inc(sem_, 1)

            def turn_ff(sem_):
                for c in range(2):
                    mm = pe.transpose(t_b[:, c * P:(c + 1) * P], act2[:, c * P:(c + 1) * P], ident)
                mm.then_inc(sem_, 1)

            def down(s0, sem_):
                w2 = view(slot_at(s0 + 2), 4, D)
                for kc in range(4):
                    for q in range(2):
                        mm = pe.matmul(dn_b[64 * q:64 * q + 64, :], ffT[:, kc % 2, 64 * (kc // 2):64 * (kc // 2) + 64],
                                       w2[:, kc, 512 * q:512 * q + 512], start=(kc == 0), stop=(kc == 3),
                                       tile_position=(0, 64 * q))
                mm.then_inc(sem_, 1)

            with pe.Fori(0, NE // 2) as i:
                for b in range(2):
                    e = i * 2 + b
                    s0 = 3 * b
                    for s in range(s0, s0 + 2):
                        pe.wait_ge(landed[s], i * 16 + 16 * (before_experts[s] + 1))
                    pe.wait_ge(hs_ready, e + 1)
                    up(hs[b], s0, up_done)
                    pe.wait_ge(ff_ready, e + 1)
                    turn_ff(ff_turned)
                    pe.wait_ge(landed[s0 + 2], i * 16 + 16 * (before_experts[s0 + 2] + 1))
                    pe.wait_ge(ffT_ready, e + 1)
                    down(s0, down_done)
                    any_extra = pe.value_load(extra_flag[0:1, :, :].rearrange("p e t -> p (e t)")[:, bass.ds(e * EXTRA, 1)],
                                               min_val=0, max_val=1)
                    with pe.If(any_extra > 0):
                        with pe.Fori(0, EXTRA) as t:
                            n = e * EXTRA + t
                            flag = pe.value_load(extra_flag[0:1, :, :].rearrange("p e t -> p (e t)")[:, bass.ds(n, 1)],
                                                 min_val=0, max_val=1)
                            with pe.If(flag > 0):
                                pe.wait_ge(x_sel, n + 1)
                                for k in range(KC):
                                    for tt in range(TT):
                                        mm = pe.matmul(xg_b[:, k * CAP:(k + 1) * CAP], xn2[:, tt, k * P:(k + 1) * P],
                                                       sel_x[:, tt, :], start=(tt == 0), stop=(tt == TT - 1))
                                mm.then_inc(x_gath, 1)
                                pe.wait_ge(x_h, n + 1)
                                up(hs_x, s0, x_up)
                                pe.wait_ge(x_ff, n + 1)
                                turn_ff(x_turned)
                                pe.wait_ge(x_ffT, n + 1)
                                down(s0, x_down)
                            with pe.Else():
                                pe.drain().then_inc(x_gath, 1)
                                pe.drain().then_inc(x_up, 1)
                                pe.drain().then_inc(x_turned, 1)
                                pe.drain().then_inc(x_down, 1)
                    with pe.Else():
                        pe.sem_inc(x_gath, EXTRA)
                        pe.sem_inc(x_up, EXTRA)
                        pe.sem_inc(x_turned, EXTRA)
                        pe.sem_inc(x_down, EXTRA)
            for i in range(4):
                banks.filled(f"moe{i}", pe.drain())

            def ab_columns(use, order):
                turn(use, view(HIGH, 4, D))
                wait_turned(use)
                for t in order:
                    project(f"c{t}", "ab0", 0, 512, t, hT, c_ready, AB_AT[t] + 1)
                for t in order:
                    pe.wait_ge(c_ready, AB_AT[t] + 1)
                    ps = banks.open(pe, f"cT{t}", c_copied, AB_AT[t] + 1)
                    for i in range(4):
                        mm = pe.transpose(ps[:, i * P:(i + 1) * P], cn[:, t % 2, i * P:(i + 1) * P], ident)
                    banks.filled(f"cT{t}", mm)
                    project(f"pj0_{t}", "ab1", 0, 512, t, hT, pj0_ready, AB_AT[t] + 1)
                for t in order:
                    project(f"pj1_{t}", "ab2", 0, 288, t, hT, pj_ready, AB_AT[t] + 1)

            ab_columns(2, AB_ORDER[0:2])
            ab_columns(3, AB_ORDER[2:4])

            def queries_keys(t):
                pe.wait_ge(c_copied, AB_AT[t] + 1)
                for g in range(2):
                    project(f"qa{t}{g}", "uq", 384 * g, 384, t, cT, qa_copied, 2 * AB_AT[t] + g + 1)
                for g in range(2):
                    name = f"kv{t}{g}"
                    pe.wait_ge(ukv_in, 16)
                    ps = banks.open(pe, name, kv_copied, 2 * AB_AT[t] + g + 1)
                    for k in range(2):
                        mm = pe.matmul(ps[:, :], cT[:, 2 + k, t * P:(t + 1) * P], w_ukv[:, k, 512 * g:512 * g + 512],
                                       start=(k == 0), stop=(k == 1))
                    banks.filled(name, mm)
                    last_use["uq"] = name

            def turn_grouped(t):
                pe.wait_ge(gqk_ready, AB_AT[t] + 1)
                ps = banks.open(pe, f"gqT{t}", gqkT_ready, 2 * AB_AT[t] + 1)
                for i in range(4):
                    mm = pe.transpose(ps[:, i * P:(i + 1) * P], pj[:, t, 32 + i * P:32 + (i + 1) * P], ident)
                banks.filled(f"gqT{t}", mm)
                ps = banks.open(pe, f"gkT{t}", gqkT_ready, 2 * AB_AT[t] + 2)
                mm = pe.transpose(ps[:, 0:P], pj[:, t, 544:672], ident)
                banks.filled(f"gkT{t}", mm)

            def turn_latent(t):
                n = AB_AT[t]
                pe.wait_ge(qk_ready, n + 1)
                for which, src in ((0, q_t), (1, k_t)):
                    for g in range(2):
                        name = f"qkT{t}{which}{g}"
                        ps = banks.open(pe, name, qkT_ready, 4 * n + 2 * which + g + 1)
                        for i in range(4):
                            mm = pe.transpose(ps[0:MD, i * P:(i + 1) * P], src[n % 2][:, 4 * g + i, :], ident)
                        banks.filled(name, mm)
                last_use["scratch"] = name

            for what, n in AB_STEPS:
                t = AB_ORDER[n % 4]
                if what == "project":
                    queries_keys(t)
                elif what == "gates":
                    project(f"ga{n // 4}_{t}", f"ab{3 + n // 4}", 0, 512, t, hT, ga_copied, n + 1)
                elif what == "grouped":
                    turn_grouped(t)
                elif what == "latent":
                    turn_latent(t)

            def attention(units, base, ops, tail, between):
                def scores(n):
                    q, k, _, keys = ops(units[n])
                    ps = banks.open(pe, f"s{base + n}", s_exp, base + n + 1)
                    nk = keys[1] - keys[0]
                    mm = pe.matmul(ps[:, 0:nk], q, k, start=True, stop=True)
                    banks.filled(f"s{base + n}", mm)

                def rest(n):
                    _, _, v, keys = ops(units[n])
                    nt = (keys[1] - keys[0]) // P
                    u = base + n
                    pe.wait_ge(s_exp, u + 1)
                    s = (pT_a, pT_v)[u % 2]
                    ps = banks.open(pe, f"p{u}", s, u // 2 + 1)
                    for i in range(nt):
                        mm = pe.transpose(ps[:, i * P:(i + 1) * P], prob[u % 3][:, i * P:(i + 1) * P], ident)
                    banks.filled(f"p{u}", mm)

                def values(n):
                    _, _, v, keys = ops(units[n])
                    nt = (keys[1] - keys[0]) // P
                    u = base + n
                    pe.wait_ge((pT_a, pT_v)[u % 2], u // 2 + 1)
                    ps = banks.open(pe, f"av{u}", mixed, u + 1)
                    for i in range(nt):
                        mm = pe.matmul(ps[:, 0:64], probT[u % 3][:, i * P:(i + 1) * P], v(keys[0] // P + i),
                                       start=(i == 0), stop=(i == nt - 1))
                    banks.filled(f"av{u}", mm)

                scores(0)
                scores(1)
                for n in range(len(units)):
                    rest(n)
                    if n + 2 < len(units):
                        scores(n + 2)
                    if n >= 1:
                        values(n - 1)
                    between(n)
                values(len(units) - 1)

            def ab_ops(unit):
                kind, h, t = unit
                keys = (0, 512) if t < TT else (T, 512)
                if kind == "m":
                    return (QT[0:MD, h, t * P:(t + 1) * P], KT[0:MD, h, keys[0]:keys[1]],
                            lambda kt: VA[:, kt, h * MV:(h + 1) * MV], keys)
                kv, g = h // GPK, h % GPK
                r = slice(64 * kv, 64 * kv + 64)
                return (qbT[r, g, t * P:(t + 1) * P], kbT[r, keys[0]:keys[1]],
                        lambda kt: VB[:, kt, kv * GD:(kv + 1) * GD], keys)

            pe.wait_ge(qkT_ready, 16)
            pe.wait_ge(gqkT_ready, 8)
            pe.wait_ge(pj_ready, 4)
            pe.wait_ge(kv_copied, 8)

            def ab_between(n):
                if n % 8 == 4 and n // 8 < 6:
                    mod(18 + n // 8)
                if n == 60:
                    mod_flush()

            attention(AB_UNITS, 0, ab_ops, None, ab_between)
            gate(2)
            gate(3)
            pe.wait_ge(mixed, NU)
            for t in range(4):
                for g in range(2):
                    name = f"mixT{t}{g}"
                    ps = banks.open(pe, name, mixT_ready, 2 * t + g + 1)
                    for i in range(4):
                        c = 4 * g + i
                        mm = pe.transpose(ps[:, i * P:(i + 1) * P], gates4[:, t, c * P:(c + 1) * P], ident)
                    banks.filled(name, mm)
            pe.wait_ge(mixT_ready, 8)
            for c in range(2):
                for t in range(4):
                    project(f"aby{c}{t}", f"abo{c}", 0, 512, t, mixT4, y_added, 4 + 4 * c + t + 1)

            turn(4, view(HIGH, 4, D))
            wait_turned(4)
            for t in range(TT):
                project(f"cdq{t}", "cd0", 0, 512, t, hT, cdq_ready, t + 1)
            for t in range(4):
                project(f"cdkv{t}", "cd1", 0, 256, t, hT, cdkv_ready, t + 1)
            for i, n in enumerate(("cd2", "cd3", "cd4")):
                for g in range(2):
                    project_T(f"cdT{i}{g}", n, [2 * g, 2 * g + 1], T, hT, cdT_ready, 2 * i + g + 1)
            for t in range(TT):
                project(f"cdg{t}", "cd5", 0, 512, t, hT, cdg_ready, t + 1)
            for g in range(2):
                project_T(f"cdT3{g}", "cd6", [2 * g, 2 * g + 1], T, hT, cdT_ready, 6 + g + 1)
            for t in range(4):
                pe.wait_ge(gqk_ready, 4 + t + 1)
                if t < TT:
                    ps = banks.open(pe, f"wqT{t}", gqkT_ready, 8 + t + 1)
                    for i in range(4):
                        mm = pe.transpose(ps[:, i * P:(i + 1) * P], cq_sb[:, t, i * P:(i + 1) * P], ident)
                    banks.filled(f"wqT{t}", mm)
            ps = banks.open(pe, "wkT", gqkT_ready, 11)
            for t in range(4):
                mm = pe.transpose(ps[:, t * P:(t + 1) * P], ckv_sb[:, t, 0:P], ident)
            banks.filled("wkT", mm)
            pe.wait_ge(gqkT_ready, 11)

            def cd_ops(unit):
                _, h, t = unit
                kv, g = h // GPK, h % GPK
                r = slice(64 * kv, 64 * kv + 64)
                return (qwT[r, g, t * P:(t + 1) * P], kwT[r, 0:512],
                        lambda kt: ckv_sb[:, kt, P + kv * GD:P + (kv + 1) * GD], (0, 512))

            attention(CD_UNITS, NU, cd_ops, None, lambda n: None)
            gate(4)
            pe.wait_ge(mixed, NU + len(CD_UNITS))
            for t in range(TT):
                name = f"cmixT{t}"
                ps = banks.open(pe, name, mixT_ready, 8 + t + 1)
                for i in range(4):
                    mm = pe.transpose(ps[:, i * P:(i + 1) * P], ga_sb[:, t, i * P:(i + 1) * P], ident)
                banks.filled(name, mm)
            pe.wait_ge(mixT_ready, 10)
            pe.wait_ge(cd_conv, 1)
            for c in range(2):
                for t in range(TT):
                    project(f"cdy{c}{t}", f"cdo{c}", 0, 512, t, mixT2, y_added, 12 + 2 * c + t + 1)

        @block.sync
        def _(sp):
            sp.dma_start(X[:, 0:2, :], a["x"][0].rearrange("(t p) d -> p t d", p=P)).then_inc(x_in, 16)
            sp.dma_start(X[:, 2:4, :], a["ctx"][0].rearrange("(t p) d -> p t d", p=P)).then_inc(ctx_in, 16)
            in_slot = [None] * 6

            def fill(ld):
                name, src, s, kdim, n = ld
                if in_slot[s] is not None:
                    banks.wait(sp, last_use[in_slot[s]])
                in_slot[s] = name
                sp.dma_start(view(slot_at(s), kdim, n), src).then_inc(landed[s], 16)

            for ld in loads[:N_BEFORE]:
                fill(ld)

            def fill_expert(e, b):
                s = 3 * b
                for j, w in enumerate(("w_gate_e", "w_up_e")):
                    sp.dma_start(view(slot_at(s + j), 1, KC, FF),
                                 a[w][0, bass.ds(e, 1)].rearrange("e (k p) f -> p e k f", p=P)).then_inc(landed[s + j], 16)
                sp.dma_start(view(slot_at(s + 2), 1, 4, D),
                             a["w_down_e"][0, bass.ds(e, 1)].rearrange("e (k p) f -> p e k f", p=P)).then_inc(landed[s + 2], 16)

            for s in range(3):
                if in_slot[s] is not None:
                    banks.wait(sp, last_use[in_slot[s]])
            fill_expert(0, 0)
            banks.wait(sp, "y11")
            sp.wait_ge(y_added, 4)
            fill_expert(1, 1)
            with sp.Fori(1, NE // 2) as i:
                for b in range(2):
                    e = i * 2 + b
                    sp.wait_ge(down_done, e - 1)
                    sp.wait_ge(x_down, e * EXTRA - EXTRA)
                    fill_expert(e, b)
            sp.wait_ge(down_done, NE - 1)
            sp.wait_ge(x_down, (NE - 1) * EXTRA)
            in_slot = [None] * 6
            for ld in loads[N_BEFORE:]:
                fill(ld)
                if ld[0] == "uq":
                    sp.dma_start(w_ukv, a["mla_w_ukv_2"][0].rearrange("(k p) c -> p k c", p=P)).then_inc(ukv_in, 16)
                if ld[0] == "ab4":
                    in_slot[2] = "scratch"
            for c in range(2):
                for t in range(TT):
                    sp.wait_ge(y_added, 12 + 2 * c + t + 1)
                    sp.dma_start(out[0, t * P:(t + 1) * P, 512 * c:512 * c + 512],
                                 X[:, t, 512 * c:512 * c + 512]).then_inc(out_sem, 16)
            sp.wait_ge(out_sem, 16 * 4)

        @block.scalar
        def _(act):
            steps = [0]

            def link(ins):
                steps[0] += 1
                ins.then_inc(a_step, 1)
                act.wait_ge(a_step, steps[0])

            act.dma_start(con[:, :], a["constants"]).then_inc(con_in, 16)
            for n, r, half in row_list:
                s = row_at[n][0]
                src = a[n]
                nd = len(src.shape)
                names = "abcd"[:nd]
                flat = src.rearrange("%s -> (%s)" % (" ".join(names), " ".join(names))) if nd > 1 else src
                act.dma_start(rows_sb[s:s + r, half, :], flat.rearrange("(r c) -> r c", c=P)).then_inc(rows_in, 16)
            for z in range(2):
                act.dma_start(gate_a[:, :, z, :], a["gla_w_gate_a"][0, z].rearrange("(k p) r -> p k r", p=P))\
                   .then_inc(small_w_in, 16)
            act.dma_start(w_route[:, :, :], a["w_router"].rearrange("(k p) e -> p k e", p=P)).then_inc(small_w_in, 16)
            for z in range(2):
                act.dma_start(gate_b[0:GATE_RANK, z, :], a["gla_w_gate_b"][0, z]).then_inc(gate_b_in, 16)

            def norm(use, junk, ins_done):
                ts = NORM_TILES[use]
                for t in ts:
                    ins_done(t)
                    ins = act.activation(junk[:, t, :], X[:, t, :], ACT.Square, accum_out=sums[:, t:t + 1])
                link(ins)
                act.preload_act_table_set(LN_EXP)
                rs = rstd[:, ts[0]:ts[-1] + 1]
                link(act.activation(rs, sums[:, ts[0]:ts[-1] + 1], ACT.Ln, bias=eps, scale=1.0 / D))
                act.activation(rs, rs, ACT.Exp, scale=-0.5).then_inc(rstd_ready, 1)

            def mod(m):
                ps = banks.wait(act, f"row{m}")
                if m >= 2:
                    banks.wait(act, f"col{m - 2}")
                act.activation(mod_rows[:, m % 2, :], ps[:, :], ACT.Copy).then_inc(row_ready, 1)

            def turn(use, dst, cs):
                act.wait_ge(coef_ready, max(c for _, _, c in cs) + 1)
                for k in range(0, KC, 2):
                    ps = banks.wait(act, f"turn{use}_{k}")
                    for lo, hi, c in cs:
                        ins = act.activation(dst[:, k, lo:hi], ps[:, lo:hi], ACT.Identity,
                                             bias=coef[:, c, 1, k:k + 1], scale=coef[:, c, 0, k:k + 1])
                    ins.then_inc(turned_a, 1)

            def gate(u):
                for h in range(2):
                    ps = banks.wait(act, f"gate{u}_{h}")
                    if u == 0 and h == 0:
                        act.wait_ge(rows_zeroed, 16 * NE)
                    act.activation(gate_rows[:, u % 2, 512 * h:512 * h + 512], ps[:, :], ACT.Copy).then_inc(gate_bc, 1)

            act.wait_ge(cols_ready, 2)
            act.wait_ge(silu_zeroed, 1)
            for m, n in enumerate(("c", "c_ctx", "c_2", "c_ctx_2")):
                act.activation(silu_c[:, m // 2, :, m % 2], column(n), ACT.Silu).then_inc(silu_ready, 1)

            def arrived(t):
                act.wait_ge(x_in if t < TT else ctx_in, 16)

            norm(0, xn, arrived)
            for m in range(4):
                mod(m)
            turn(0, hT, [(0, T, 0), (T, 512, 1)])
            for h in range(HG):
                ps = banks.wait(act, f"k{h}")
                act.activation(kT[:, h, :], ps[:, :], ACT.Copy).then_inc(k_ready, 1)
            mod(4)
            for g in range(2):
                ps = banks.wait(act, f"q{g}")
                act.activation(qT[:, 2 * g:2 * g + 2, :], ps[:, :].rearrange("p (h t) -> p h t", h=2), ACT.Copy,
                               scale=float(DK) ** -0.5).then_inc(q_ready, 1)
            mod(5)
            for z in range(2):
                ps = banks.wait(act, f"low{z}")
                act.activation(low[0:GATE_RANK, z, :], ps[0:GATE_RANK, :], ACT.Copy).then_inc(low_ready, 1)
            for z in range(2):
                act.wait_ge(z_ready, 4 * z + 4)
                link(act.activation(zt[:, z], zg[:, z], ACT.Abs))
                act.preload_act_table_set(LN_EXP)
                link(act.activation(zt[:, z], zt[:, z], ACT.Exp, scale=-1.0))
                act.activation(zt[:, z], zt[:, z], ACT.Ln, bias=ones[:, 0:1]).then_inc(softplus_ready, 1)
            mod(6)
            mod(7)
            for c in range(2):
                for t in range(TT):
                    ps = banks.wait(act, f"r{c}_{t}")
                    act.activation(r_sb[:, t, 512 * c:512 * c + 512], ps[:, :], ACT.Silu).then_inc(r_ready, 1)
                mod(8 + c)
            act.preload_act_table_set(LN_EXP)
            act.wait_ge(kd_arg, 1)
            act.activation(kdT[:, 0], kdT[:, 0], ACT.Exp, scale=1.0 / GATE_NORM)
            act.activation(kdT[:, 1], cum[:, 1, :, 1, 0:T], ACT.Exp, scale=1.0 / GATE_NORM).then_inc(kd_exp, 1)
            act.wait_ge(qd_arg, 1)
            act.activation(qdec[0], cum[:, 0, :, 0, 1:T + 1], ACT.Exp, scale=1.0 / GATE_NORM)
            act.activation(qdec[1], qdec[1], ACT.Exp, scale=1.0 / GATE_NORM).then_inc(qd_exp, 1)
            for g in range(4):
                ps = banks.wait(act, f"kd{g}")
                z, h0 = g // 2, 2 * (g % 2)
                act.activation(kd[:, z, h0:h0 + 2].rearrange("p h t d -> p (h t) d"),
                               ps[:, :].rearrange("p (a d) -> p a d", a=4), ACT.Copy).then_inc(kd_turned, 1)

            def level_exp(li):
                act.wait_ge(lev_arg, li + 1)
                L = lev[(li + 1) % 2]
                act.activation(L, L, ACT.Exp, scale=1.0 / GATE_NORM).then_inc(lev_exp, 1)

            level_exp(0)
            for g in range(4):
                ps = banks.wait(act, f"state{g}")
                act.activation(S_sb[:, 2 * g:2 * g + 2, :], ps[:, :].rearrange("p (a d) -> p a d", a=2), ACT.Copy)\
                   .then_inc(state_ready, 1)
            for li in range(len(LEVELS)):
                if li + 1 < len(LEVELS):
                    level_exp(li + 1)
                if li == 0:
                    for g in range(2):
                        ps = banks.wait(act, f"off{g}")
                        act.activation(sc_off[:, 2 * g:2 * g + 2].rearrange("p h s i -> p (h s) i"),
                                       ps[:, :].rearrange("p (a i) -> p a i", a=4), ACT.Copy).then_inc(off_ready, 1)
                mod(10 + li)
            act.wait_ge(o_copied, 4)
            for t in range(TT):
                for h in range(HG):
                    ins = act.activation(oT[:, HG * t + h, :], o_sb[:, t, h * DV:(h + 1) * DV], ACT.Square,
                                         accum_out=sums[:, HG * t + h:HG * t + h + 1])
            link(ins)
            link(act.activation(rstd[:, 0:8], sums[:, 0:8], ACT.Ln, bias=eps, scale=1.0 / DV))
            act.activation(rstd[:, 0:8], rstd[:, 0:8], ACT.Exp, scale=-0.5).then_inc(o_rstd, 1)
            gate(0)
            for g in range(4):
                ps = banks.wait(act, f"oT{g}")
                act.activation(oT[:, 2 * g:2 * g + 2, :], ps[:, :].rearrange("p (c t) -> p c t", c=2), ACT.Copy)\
                   .then_inc(oT_ready, 1)
            act.wait_ge(y_added, 4)
            norm(1, xn2, lambda t: None)
            turn(1, h2T, [(0, T, 2)])
            ps = banks.wait(act, "logits")
            act.activation(small[:, 0:32], ps[:, 0:32], ACT.Exp, scale=-1.0).then_inc(logit_exp, 1)
            gate(1)
            for half in range(2):
                for k in range(0, KC, 2):
                    ps = banks.wait(act, f"gath{half}_{k}")
                    act.activation(hg[:, k, 512 * half:512 * half + 512], ps[:, :], ACT.Identity,
                                   bias=coef[:, 2, 1, k:k + 1], scale=coef[:, 2, 0, k:k + 1]).then_inc(hg_a, 1)
            act.preload_act_table(ACT.Silu)
            act.wait_ge(rows_zeroed, 16 * NE)
            for b in range(2):
                act.sem_inc(stored[b], 32)
            act.sem_inc(x_stored, 32)
            n_moe = [banks.at[f"moe{i}"] % 8 for i in range(4)]
            up_b, t_b, dn_b, xg_b = [banks.banks[n] for n in n_moe]

            def store(buf, row0, sem_):
                for q in range(2):
                    act.dma_start(y_rows[bass.ds(row0, CAP), 512 * q:512 * q + 512], buf[64 * q:64 * q + 64, :])\
                       .then_inc(sem_, 16)

            with act.Fori(0, NE // 2) as i:
                for b in range(2):
                    e = i * 2 + b
                    act.wait_ge(up_done, e + 1)
                    act.activation(act1, up_b[:, 0:256], ACT.Silu).then_inc(silu_done, 1)
                    act.wait_ge(ff_turned, e + 1)
                    act.activation(ffT, t_b[:, 0:256].rearrange("p (c s) -> p c s", c=2), ACT.Copy).then_inc(ffT_ready, 1)
                    act.wait_ge(ye_ready, e + 1)
                    store(y_buf[b], e * T, stored[b])
                    any_extra = act.value_load(extra_flag[0:1, :, :].rearrange("p e t -> p (e t)")[:, bass.ds(e * EXTRA, 1)],
                                               min_val=0, max_val=1)
                    with act.If(any_extra > 0):
                        with act.Fori(0, EXTRA) as t:
                            n = e * EXTRA + t
                            flag = act.value_load(extra_flag[0:1, :, :].rearrange("p e t -> p (e t)")[:, bass.ds(n, 1)],
                                                  min_val=0, max_val=1)
                            with act.If(flag > 0):
                                act.wait_ge(x_gath, n + 1)
                                for k in range(KC):
                                    ins = act.activation(hs_x[:, k, :], xg_b[:, k * CAP:(k + 1) * CAP], ACT.Identity,
                                                         bias=coef[:, 2, 1, k:k + 1], scale=coef[:, 2, 0, k:k + 1])
                                ins.then_inc(x_h, 1)
                                act.wait_ge(x_up, n + 1)
                                act.activation(act1, up_b[:, 0:256], ACT.Silu).then_inc(x_silu, 1)
                                act.wait_ge(x_turned, n + 1)
                                act.activation(ffT, t_b[:, 0:256].rearrange("p (c s) -> p c s", c=2), ACT.Copy)\
                                   .then_inc(x_ffT, 1)
                                act.wait_ge(x_ye, n + 1)
                                store(y_x, e * T + t * CAP + CAP, x_stored)
                            with act.Else():
                                act.sem_inc(x_h, 1)
                                act.sem_inc(x_silu, 1)
                                act.sem_inc(x_ffT, 1)
                                act.sem_inc(x_stored, 32)

                    with act.Else():
                        act.sem_inc(x_h, EXTRA)
                        act.sem_inc(x_silu, EXTRA)
                        act.sem_inc(x_ffT, EXTRA)
                        act.sem_inc(x_stored, 32 * EXTRA)
            act.wait_ge(y_added, 4)
            act.wait_ge(experts_done, 1)
            act.wait_ge(ctx2_in, 16)
            norm(2, view(HIGH, 4, D), lambda t: None)
            for b in range(2):
                act.wait_ge(stored[b], 32 * (NE // 2 + 1))
            act.wait_ge(x_stored, 32 * (NE * EXTRA + 1))

            def ab_columns(use, order, cs):
                turn(use, hT, cs)
                for t in order:
                    ps = banks.wait(act, f"c{t}")
                    for g in range(2):
                        ins = act.activation(gates4[:, 0, RANK * g:RANK * g + RANK], ps[:, RANK * g:RANK * g + RANK],
                                             ACT.Square, accum_out=sums[:, 16 + 2 * t + g:16 + 2 * t + g + 1])
                    link(ins)
                    rs = rstd[:, 16 + 2 * t:16 + 2 * t + 2]
                    link(act.activation(rs, sums[:, 16 + 2 * t:16 + 2 * t + 2], ACT.Ln, bias=eps, scale=1.0 / RANK))
                    act.activation(rs, rs, ACT.Exp, scale=-0.5).then_inc(c_ms, 1)
                for t in order:
                    ps = banks.wait(act, f"cT{t}")
                    act.activation(cT[:, :, t * P:(t + 1) * P], ps[:, :].rearrange("p (c t) -> p c t", c=4), ACT.Copy)\
                       .then_inc(c_copied, 1)
                    ps = banks.wait(act, f"pj0_{t}")
                    act.activation(pj[:, t, 0:512], ps[:, :], ACT.Copy).then_inc(pj0_ready, 1)
                for t in order:
                    ps = banks.wait(act, f"pj1_{t}")
                    act.activation(pj[:, t, 512:672], ps[:, 0:160], ACT.Copy)
                    act.activation(VB[:, t, :], ps[:, 160:288], ACT.Copy).then_inc(pj_ready, 1)

            def head_rstd(o, n, dq, logq, nq, nk):
                act.wait_ge(qk_ms, n + 1)
                link(act.activation(rstd[:, o:o + nq + nk], sums[:, o:o + nq + nk], ACT.Ln, bias=eps, scale=1.0 / dq))
                if nq:
                    act.activation(rstd[:, o:o + nq], rstd[:, o:o + nq], ACT.Exp, scale=-0.5, bias=logq)
                act.activation(rstd[:, o + nq:o + nq + nk], rstd[:, o + nq:o + nq + nk], ACT.Exp, scale=-0.5)\
                   .then_inc(qk_rstd, 1)

            ab_columns(2, AB_ORDER[0:2], [(T, 512, 4)])
            for n in range(2):
                head_rstd(32, n, GD, log_q_gqa, GH, KVH)
            act.wait_ge(x_moe, 2)
            norm(3, y_tok[:, :, 0, :], lambda t: None)
            act.wait_ge(block1_done, 2)
            norm(4, view(HIGH, 4, D), lambda t: None)
            ab_columns(3, AB_ORDER[2:4], [(0, T, 3)])

            for what, n in AB_STEPS:
                t = AB_ORDER[n % 4]
                if what == "project":
                    for g in range(2):
                        ps = banks.wait(act, f"qa{t}{g}")
                        if n >= 2:
                            banks.wait(act, f"qkT{AB_ORDER[n - 2]}01")
                        act.activation(q_t[n % 2][:, 4 * g:4 * g + 4, :], ps[:, 0:384].rearrange("p (h d) -> p h d", h=4),
                                       ACT.Copy).then_inc(qa_copied, 1)
                    for g in range(2):
                        ps = banks.wait(act, f"kv{t}{g}")[:, :].rearrange("p (h d) -> p h d", h=4)
                        if n >= 2:
                            banks.wait(act, f"qkT{AB_ORDER[n - 2]}11")
                        act.activation(k_t[n % 2][:, 4 * g:4 * g + 4, 0:NOPE], ps[:, :, 0:NOPE], ACT.Copy)
                        act.activation(VA[:, t, 4 * MV * g:4 * MV * g + 4 * MV].rearrange("p (h d) -> p h d", h=4),
                                       ps[:, :, NOPE:P], ACT.Copy).then_inc(kv_copied, 1)
                elif what == "gates":
                    ps = banks.wait(act, f"ga{n // 4}_{t}")
                    c = n // 4
                    act.activation(gates4[:, t, 512 * c:512 * c + 512], ps[:, :], ACT.Copy).then_inc(ga_copied, 1)
                elif what == "grouped norm":
                    head_rstd(32, n, GD, log_q_gqa, GH, KVH)
                elif what == "latent norm":
                    head_rstd(0, 4 + n, MD, log_q_mla, MH, MH)
                elif what == "grouped":
                    ps = banks.wait(act, f"gqT{t}")
                    act.activation(qbT[:, :, t * P:(t + 1) * P], ps[:, :].rearrange("p (g t) -> p g t", g=4), ACT.Copy)\
                       .then_inc(gqkT_ready, 1)
                    ps = banks.wait(act, f"gkT{t}")
                    act.activation(kbT[:, t * P:(t + 1) * P], ps[:, 0:P], ACT.Copy).then_inc(gqkT_ready, 1)
                elif what == "latent":
                    if n == 0:
                        act.wait_ge(gqk_ready, 4)
                    for which, dst in ((0, QT), (1, KT)):
                        for g in range(2):
                            ps = banks.wait(act, f"qkT{t}{which}{g}")
                            act.activation(dst[0:MD, 4 * g:4 * g + 4, t * P:(t + 1) * P],
                                           ps[0:MD, :].rearrange("p (h t) -> p h t", h=4), ACT.Copy).then_inc(qkT_ready, 1)
            act.wait_ge(ga_copied, 8)
            act.preload_act_table(ACT.Silu)
            for t in range(4):
                act.activation(gates4[:, t, :], gates4[:, t, :], ACT.Silu).then_inc(gate4_ready, 1)
            act.preload_act_table_set(LN_EXP)

            def attention(units, base, nkeys, between, sink):
                def exps(n):
                    u = base + n
                    ps = banks.wait(act, f"s{u}")
                    act.wait_ge(s_max, u + 1)
                    if n >= 3:
                        banks.wait(act, f"p{u - 3}")
                    if sink:
                        h = units[n][1]
                        link(act.activation(small[:, 528 + u % 4:529 + u % 4], gain["win_sink_2"][:, h:h + 1], ACT.Exp,
                                            bias=small[:, 512 + u % 4:513 + u % 4]))
                    act.activation(prob[u % 3][:, 0:nkeys(n)], ps[:, 0:nkeys(n)], ACT.Exp,
                                   bias=small[:, 512 + u % 4:513 + u % 4],
                                   accum_out=small[:, 520 + u % 4:521 + u % 4]).then_inc(s_exp, 1)

                def turned(n):
                    u = base + n
                    if u % 2 == 0:
                        ps = banks.wait(act, f"p{u}")
                        if n >= 3:
                            banks.wait(act, f"av{u - 3}")
                        act.activation(probT[u % 3][:, 0:nkeys(n)], ps[:, 0:nkeys(n)], ACT.Copy).then_inc(pT_a, 1)

                exps(0)
                for n in range(len(units)):
                    if n + 1 < len(units):
                        exps(n + 1)
                    turned(n)
                    between(n)

            def ab_between(n):
                if n % 8 == 4 and n // 8 < 6:
                    mod(18 + n // 8)

            attention(AB_UNITS, 0, lambda n: 512 if AB_UNITS[n][2] < TT else 256, ab_between, False)
            gate(2)
            gate(3)
            for t in range(4):
                for g in range(2):
                    ps = banks.wait(act, f"mixT{t}{g}")
                    act.activation(mixT4[:, 4 * g:4 * g + 4, t * P:(t + 1) * P],
                                   ps[:, :].rearrange("p (c t) -> p c t", c=4), ACT.Copy).then_inc(mixT_ready, 1)
            act.wait_ge(y_added, 12)
            norm(5, view(HIGH, 4, D), lambda t: None)
            turn(4, hT, [(0, T, 5), (T, 512, 6)])
            for t in range(TT):
                ps = banks.wait(act, f"cdq{t}")
                act.activation(cq_sb[:, t, :], ps[:, :], ACT.Copy).then_inc(cdq_ready, 1)
            for t in range(4):
                ps = banks.wait(act, f"cdkv{t}")
                act.activation(ckv_sb[:, t, :], ps[:, 0:256], ACT.Copy).then_inc(cdkv_ready, 1)
            for t in range(4):
                head_rstd(32, 8 + t, GD, log_q_gqa, GH if t < TT else 0, KVH)
            for i, dst in enumerate((gbT, gcT, ghT)):
                for g in range(2):
                    ps = banks.wait(act, f"cdT{i}{g}")
                    act.activation(dst[:, 2 * g:2 * g + 2, :], ps[:, :].rearrange("p (c t) -> p c t", c=2), ACT.Copy)\
                       .then_inc(cdT_ready, 1)
            for t in range(TT):
                ps = banks.wait(act, f"cdg{t}")
                act.activation(ga_sb[:, t, :], ps[:, :], ACT.Silu).then_inc(cdg_ready, 1)
            for g in range(2):
                ps = banks.wait(act, f"cdT3{g}")
                act.activation(gaT[:, 2 * g:2 * g + 2, :], ps[:, :].rearrange("p (c t) -> p c t", c=2), ACT.Silu)\
                   .then_inc(cdT_ready, 1)
            act.preload_act_table_set(LN_EXP)
            for t in range(TT):
                ps = banks.wait(act, f"wqT{t}")
                act.activation(qwT[:, :, t * P:(t + 1) * P], ps[:, :].rearrange("p (g t) -> p g t", g=4), ACT.Copy)\
                   .then_inc(gqkT_ready, 1)
            ps = banks.wait(act, "wkT")
            act.activation(kwT[:, :], ps[:, :], ACT.Copy).then_inc(gqkT_ready, 1)
            attention(CD_UNITS, NU, lambda n: 512, lambda n: None, True)
            gate(4)
            for t in range(TT):
                ps = banks.wait(act, f"cmixT{t}")
                act.activation(mixT2[:, 0:4, t * P:(t + 1) * P], ps[:, :].rearrange("p (c t) -> p c t", c=4), ACT.Copy)\
                   .then_inc(mixT_ready, 1)

        @block.vector
        def _(dve):
            steps = [0]

            def link(ins):
                steps[0] += 1
                ins.then_inc(v_step, 1)
                dve.wait_ge(v_step, steps[0])

            def small_at(s, *dims):
                n = int(np.prod(dims))
                v = small[:, s:s + n]
                if len(dims) == 1:
                    return v
                names = "abc"[:len(dims)]
                return v.rearrange("p (%s) -> p %s" % (" ".join(names), " ".join(names)),
                                   **{names[i]: dims[i] for i in range(len(dims))})

            def inner(ap, n):
                return ap.unsqueeze(len(ap.shape)).broadcast_to(list(ap.shape) + [n])

            def outer(ap, n):
                return ap.unsqueeze(1).broadcast_to([ap.shape[0], n] + list(ap.shape[1:]))

            def norm_rows(use, dst):
                dve.wait_ge(rstd_ready, use + 1)
                for t in NORM_TILES[use]:
                    dve.tensor_scalar(dst[:, t, :], X[:, t, :], rstd[:, t:t + 1], None, ALU.mult).then_inc(xn_ready, 1)

            def mod_col(m):
                l, c = mod_chunks[m]
                ps = banks.wait(dve, f"col{m}")
                dst = mod1[:, 4 * c:4 * c + 4, :] if l == 0 else mod2[:, l - 1, 4 * c:4 * c + 4, :]
                bias = column("b_mod")[:, 4 * c:4 * c + 4] if l == 0 else \
                    column("mod_b_2")[:, 24 * (l - 1) + 4 * c:24 * (l - 1) + 4 * c + 4]
                dve.tensor_tensor(dst, ps[:, 0:8].rearrange("p (c m) -> p c m", m=2), inner(bias, 2), ALU.add)\
                   .then_inc(modcol_ready, 1)

            def coefficients(u, scale, shift, gain_col):
                if gain_col is None:
                    dve.tensor_scalar(coef[:, u, 0, :], scale, 1.0, None, ALU.add)
                else:
                    dve.scalar_tensor_tensor(coef[:, u, 0, :], scale, 1.0, gain_col, ALU.add, ALU.mult)
                dve.tensor_copy(coef[:, u, 1, :], shift).then_inc(coef_ready, 1)

            def turn(use, dst, cs):
                dve.wait_ge(coef_ready, max(c for _, _, c in cs) + 1)
                for k in range(1, KC, 2):
                    ps = banks.wait(dve, f"turn{use}_{k}")
                    for lo, hi, c in cs:
                        ins = dve.tensor_scalar(dst[:, k, lo:hi], ps[:, lo:hi], coef[:, c, 0, k:k + 1],
                                                coef[:, c, 1, k:k + 1], ALU.mult, ALU.add)
                    ins.then_inc(turned_v, 1)

            def gate(u, col):
                if u >= 1:
                    banks.wait(dve, f"gate{u - 1}_1")
                dve.tensor_tensor(gate_diag[:, :, :], outer(ident, KC), inner(col, P), ALU.mult).then_inc(diag_gate, 1)

            added = [0]

            def add_gated(name, tmp, u, c, t):
                ps = banks.wait(dve, name)
                cs = slice(512 * c, 512 * c + 512)
                if added[0]:
                    dve.wait_ge(y_added, added[0])
                added[0] += 1
                link(dve.tensor_tensor(tmp, ps[:, :], gate_rows[:, u % 2, cs], ALU.mult))
                dve.tensor_tensor(X[:, t, cs], X[:, t, cs], tmp, ALU.add).then_inc(y_added, 1)

            for half in range(2):
                ps = banks.wait(dve, f"cols{half}")
                o = half * nrow[0]
                dve.tensor_copy(colv[:, o:o + nrow[half]], ps[:, 0:nrow[half]]).then_inc(cols_ready, 1)
            dve.wait_ge(cols_ready, 2)
            norm_rows(0, xn)
            for m in range(4):
                mod_col(m)
            dve.wait_ge(modcol_ready, 4)
            for m in range(2):
                coefficients(m, mod1[:, 8:16, m], mod1[:, 0:8, m], column("norm1_g"))
            turn(0, hT, [(0, T, 0), (T, 512, 1)])
            mod_col(4)
            for t in range(2):
                ps = banks.wait(dve, f"v0_{t}")
                dve.tensor_copy(v_sb[:, t, 0:512], ps[:, :]).then_inc(v_ready, 1)
            for n in range(2 * HG):
                ps = banks.wait(dve, f"z{n}")
                dve.tensor_scalar(zg[:, n // HG, n % HG, :], ps[:, :], column("gla_b_gate")[:, n:n + 1], None, ALU.add)\
                   .then_inc(z_ready, 1)
            for t in range(2, 4):
                ps = banks.wait(dve, f"v0_{t}")
                dve.tensor_copy(v_sb[:, t, 0:512], ps[:, :]).then_inc(v_ready, 1)
            mod_col(5)
            for z in range(2):
                dve.wait_ge(softplus_ready, z + 1)
                link(dve.scalar_tensor_tensor(zg[:, z], zg[:, z], 0.0, zt[:, z], ALU.min, ALU.subtract))
            link(dve.memset(cum[:, :, :, :, 0:1].rearrange("p z h s o -> p (z h s) o"), 0.0))
            for t in range(4):
                ps = banks.wait(dve, f"v1_{t}")
                dve.tensor_copy(v_sb[:, t, 512:1024], ps[:, :]).then_inc(v_ready, 1)
                for h in range(HG):
                    z, hh = t // 2, 2 * (t % 2) + h // 2
                    s = h % 2
                    ins = dve.tensor_tensor_scan(cum[:, z, hh, s, 1:T + 1], ones256, zg[:, z, hh, s * T:(s + 1) * T], 0.0,
                                                 ALU.mult, ALU.add)
                link(ins)
            mod_col(6)
            dve.tensor_tensor(kdT[:, 0], cum[:, 0, :, 1, T:T + 1].broadcast_to([P, HG, T]), cum[:, 0, :, 1, 1:T + 1],
                              ALU.subtract).then_inc(kd_arg, 1)
            dve.tensor_tensor(qdec[1], cum[:, 1, :, 0, T:T + 1].broadcast_to([P, HG, T]), cum[:, 1, :, 0, 0:T],
                              ALU.subtract).then_inc(qd_arg, 1)
            mod_col(7)
            mod_col(8)

            def level_args(li):
                b = LEVELS[li]
                if li == 1:
                    banks.wait(dve, "kd3")
                elif li >= 2:
                    banks.wait(dve, "off1" if li == 2 else f"lev{li - 2}_1")
                L = lev[(li + 1) % 2]
                halves = "p h (n s b) -> p h n s b"
                q, k = (L[:, i].rearrange(halves, s=2, b=b) for i in range(2))
                fwd = cum[:, 0, :, 0, 1:T + 1].rearrange(halves, s=2, b=b)
                bwd = cum[:, 1, :, 0, 0:T].rearrange(halves, s=2, b=b)
                f_at, b_at = (inner(cum[:, z, :, 0, b:T + 1:2 * b], b) for z in range(2))
                dve.tensor_tensor(q[:, :, :, 1, :], fwd[:, :, :, 1, :], f_at, ALU.subtract)
                dve.tensor_tensor(q[:, :, :, 0, :], b_at, bwd[:, :, :, 0, :], ALU.subtract)
                dve.tensor_tensor(k[:, :, :, 0, :], f_at, fwd[:, :, :, 0, :], ALU.subtract)
                dve.tensor_tensor(k[:, :, :, 1, :], bwd[:, :, :, 1, :], b_at, ALU.subtract).then_inc(lev_arg, 1)

            level_args(0)
            dve.wait_ge(kd_exp, 1)
            dve.wait_ge(k_ready, HG)
            dve.wait_ge(q_ready, 2)
            dve.tensor_tensor(kdT[:, 0], kdT[:, 0], kT[:, :, T:512], ALU.mult)
            dve.tensor_tensor(kdT[:, 1], kdT[:, 1], kT[:, :, T:512], ALU.mult).then_inc(kd_ready, 1)
            dve.wait_ge(qd_exp, 1)
            for z in range(2):
                dve.tensor_tensor(qdec[z], qdec[z], qT, ALU.mult).then_inc(qd_ready, 1)
            for g in range(2):
                ps = banks.wait(dve, f"same{g}")
                dve.scalar_tensor_tensor(sc_diag[:, 4 * g:4 * g + 4, :], ps[:, :].rearrange("p (a i) -> p a i", a=4), 2.0,
                                         outer(ident, 4), ALU.mult, ALU.mult).then_inc(diag_ready, 1)
            dve.wait_ge(diag_ready, 2)
            for li in range(len(LEVELS)):
                if li + 1 < len(LEVELS):
                    level_args(li + 1)
                dve.wait_ge(lev_exp, li + 1)
                L = lev[(li + 1) % 2]
                dve.tensor_tensor(L[:, 0], L[:, 0], qT, ALU.mult)
                dve.tensor_tensor(L[:, 1], L[:, 1], kT[:, :, 0:T], ALU.mult).then_inc(lev_ready, 1)
                if li >= 1:
                    for g in range(2):
                        ps = banks.wait(dve, f"lev{li}_{g}")
                        dve.copy_predicated(sc_diag[:, 4 * g:4 * g + 4, :], outer(level_masks[:, li - 1, :], 4),
                                            ps[:, :].rearrange("p (a i) -> p a i", a=4)).then_inc(lev_used, 1)
                mod_col(9 + li)
            mod_col(17)
            for n in range(4):
                t, hp = n // 2, n % 2
                ps = banks.wait(dve, f"o{t}{hp}")
                dve.tensor_copy(o_sb[:, t, 512 * hp:512 * hp + 512], ps[:, :]).then_inc(o_copied, 1)
            dve.wait_ge(modcol_ready, 18)
            gate(0, mod1[:, 16:24, 0])
            coefficients(2, mod1[:, 32:40, 0], mod1[:, 24:32, 0], column("norm2_g"))
            for m in range(2):
                coefficients(3 + m, mod2[:, 0, 8:16, m], mod2[:, 0, 0:8, m], None)
            dve.wait_ge(o_rstd, 1)
            dve.wait_ge(r_ready, 4)
            dve.wait_ge(gains_in, 16 * len(gain_widths))
            for t in range(TT):
                for h in range(HG):
                    o = o_sb[:, t, h * DV:(h + 1) * DV]
                    ins = dve.scalar_tensor_tensor(o, o, rstd[:, HG * t + h:HG * t + h + 1], gain["gla_norm_g"],
                                                   ALU.mult, ALU.mult)
                link(ins)
                dve.tensor_tensor(o_sb[:, t, :], o_sb[:, t, :], r_sb[:, t, :], ALU.mult).then_inc(o_ready, 1)
            dve.wait_ge(gate_bc, 2)
            for c in range(2):
                for t in range(TT):
                    add_gated(f"y{c}{t}", y_t1, 0, c, t)
            norm_rows(1, xn2)
            turn(1, h2T, [(0, T, 2)])
            gate(1, mod1[:, 40:48, 0])
            score, pick, mask = small_at(32, TT, NE), small_at(64, TT, NE), small_at(96, TT, NE)
            gates_r, rank, rank_m = small_at(128, TT, NE), small_at(160, TT, NE), small_at(192, TT, NE)
            row_v, cnt = small_at(224, TT, NE), small_at(256, NE)
            wsum, rows_ab, gates_ab = small_at(272, TT), small_at(274, TT, 2), small_at(282, TT, 2)
            beat, tie = small_at(288, GROUPS, EPG, EPG), small_at(352, GROUPS, EPG, EPG)
            place = small_at(416, TT, NE)
            gscore, gplace, tmp32 = small_at(448, TT, GROUPS), small_at(456, TT, GROUPS), small_at(464, TT, NE)
            dve.wait_ge(logit_exp, 1)
            link(dve.tensor_scalar(small[:, 0:32], small[:, 0:32], 1.0, None, ALU.add))
            link(dve.reciprocal(score, small_at(0, TT, NE)))
            link(dve.tensor_tensor(pick, score, outer(gain["b_router"], TT), ALU.add))

            def places(dst, src, groups, n):
                s = src.rearrange("p (g n) -> p g n", n=n)
                mine = inner(s, n)
                theirs = s.unsqueeze(2).broadcast_to([P, groups, n, n])
                b4, t4 = beat[:, 0:groups, 0:n, 0:n], tie[:, 0:groups, 0:n, 0:n]
                dve.tensor_tensor(b4, theirs, mine, ALU.is_gt)
                link(dve.tensor_tensor(t4, theirs, mine, ALU.is_equal))
                link(dve.tensor_tensor(t4, t4, outer(earlier, groups), ALU.mult))
                link(dve.tensor_tensor(b4, b4, t4, ALU.add))
                link(dve.tensor_reduce(dst, b4.rearrange("p g i j -> p (g i) j"), AX.X, ALU.add))

            for t in range(TT):
                places(place[:, t, :], pick[:, t, :], GROUPS, EPG)
            link(dve.tensor_scalar(mask, place, 2.0, None, ALU.is_lt))
            link(dve.tensor_tensor(tmp32, pick, mask, ALU.mult))
            link(dve.tensor_reduce(gscore.rearrange("p t g -> p (t g)"),
                                   tmp32.rearrange("p t (g e) -> p (t g) e", e=EPG), AX.X, ALU.add))
            for t in range(TT):
                places(gplace[:, t, :], gscore[:, t, :], 1, GROUPS)
            link(dve.tensor_scalar(gplace, gplace, 1.0, None, ALU.is_lt))
            m3 = mask.rearrange("p t (g e) -> p (t g) e", e=EPG)
            dve.tensor_tensor(m3, m3, inner(gplace.rearrange("p t g -> p (t g)"), EPG), ALU.mult).then_inc(routed, 1)
            dve.wait_ge(routed, 1)
            link(dve.tensor_tensor(gates_r, mask, score, ALU.mult))
            link(dve.tensor_reduce(wsum, gates_r, AX.X, ALU.add))
            link(dve.reciprocal(wsum, wsum))
            link(dve.tensor_tensor(gates_r, gates_r, inner(wsum, NE), ALU.mult))
            ps = banks.wait(dve, "ranks")
            dve.tensor_copy(cnt, ps[:, 2 * NE:3 * NE])
            dve.tensor_copy(rank, ps[:, 0:2 * NE].rearrange("p (t e) -> p t e", t=TT)).then_inc(ranked, 1)
            dve.wait_ge(ranked, 1)
            for t in range(EXTRA):
                dve.tensor_scalar(extra_flag[:, :, t], cnt, float(CAP * (t + 1)), None, ALU.is_gt)
            link(dve.scalar_tensor_tensor(rank_m, rank, 1.0, mask, ALU.add, ALU.mult))
            link(dve.tensor_scalar(rank_m, rank_m, -1.0, None, ALU.add))
            for t in range(TT):
                dve.tensor_tensor(sel[:, t, :].rearrange("p (e s) -> p e s", s=CAP), outer(iota[:, 0:CAP], NE),
                                  inner(rank_m[:, t, :], CAP), ALU.is_equal).then_inc(sel_ready, 1)
            link(dve.tensor_tensor(row_v, rank, outer(row_base, TT), ALU.add))
            big = 2.0 * NE * T
            link(dve.scalar_tensor_tensor(tmp32, row_v, -big, mask, ALU.add, ALU.mult))
            link(dve.tensor_reduce(rows_ab[:, :, 0], tmp32, AX.X, ALU.min))
            link(dve.tensor_scalar(rows_ab[:, :, 0], rows_ab[:, :, 0], big, None, ALU.add))
            link(dve.tensor_tensor(tmp32, row_v, mask, ALU.mult))
            link(dve.tensor_reduce(rows_ab[:, :, 1], tmp32, AX.X, ALU.max))
            for j in range(2):
                link(dve.tensor_tensor(tmp32, row_v, inner(rows_ab[:, :, j], NE), ALU.is_equal))
                link(dve.tensor_tensor(tmp32, tmp32, gates_r, ALU.mult))
                link(dve.tensor_reduce(gates_ab[:, :, j], tmp32, AX.X, ALU.add))
            link(dve.tensor_copy(route_idx[:, :, :], rows_ab))
            for half in range(2):
                for k in range(1, KC, 2):
                    ps = banks.wait(dve, f"gath{half}_{k}")
                    dve.tensor_scalar(hg[:, k, 512 * half:512 * half + 512], ps[:, :], coef[:, 2, 0, k:k + 1],
                                      coef[:, 2, 1, k:k + 1], ALU.mult, ALU.add).then_inc(hg_v, 1)
            up_b, t_b, dn_b, xg_b = [banks.banks[banks.at[f"moe{i}"] % 8] for i in range(4)]
            with dve.Fori(0, NE // 2) as i:
                for b in range(2):
                    e = i * 2 + b
                    dve.wait_ge(up_done, e + 1)
                    dve.wait_ge(silu_done, e + 1)
                    dve.tensor_tensor(act2, act1, up_b[:, 256:512], ALU.mult).then_inc(ff_ready, 1)
                    dve.wait_ge(down_done, e + 1)
                    dve.wait_ge(stored[b], i * 32 + 32)
                    dve.tensor_copy(y_buf[b], dn_b[:, :]).then_inc(ye_ready, 1)
                    any_extra = dve.value_load(extra_flag[0:1, :, :].rearrange("p e t -> p (e t)")[:, bass.ds(e * EXTRA, 1)],
                                               min_val=0, max_val=1)
                    with dve.If(any_extra > 0):
                        with dve.Fori(0, EXTRA) as t:
                            n = e * EXTRA + t
                            flag = dve.value_load(extra_flag[0:1, :, :].rearrange("p e t -> p (e t)")[:, bass.ds(n, 1)],
                                                  min_val=0, max_val=1)
                            with dve.If(flag > 0):
                                for tt in range(TT):
                                    ins = dve.tensor_scalar(sel_x[:, tt, :], iota[:, bass.ds(t * CAP + CAP, CAP)],
                                                            rank_m[:, tt, bass.ds(e, 1)], None, ALU.is_equal)
                                ins.then_inc(x_sel, 1)
                                dve.wait_ge(x_up, n + 1)
                                dve.wait_ge(x_silu, n + 1)
                                dve.tensor_tensor(act2, act1, up_b[:, 256:512], ALU.mult).then_inc(x_ff, 1)
                                dve.wait_ge(x_down, n + 1)
                                dve.wait_ge(x_stored, n * 32 + 32)
                                dve.tensor_copy(y_x, dn_b[:, :]).then_inc(x_ye, 1)
                            with dve.Else():
                                dve.sem_inc(x_sel, 1)
                                dve.sem_inc(x_ff, 1)
                                dve.drain().then_inc(x_ye, 1)
                    with dve.Else():
                        dve.sem_inc(x_sel, EXTRA)
                        dve.sem_inc(x_ff, EXTRA)
                        dve.sem_inc(x_ye, EXTRA)
            dve.drain().then_inc(experts_done, 1)
            def latent_norms(order):
                for t in order:
                    n = AB_AT[t]
                    dve.wait_ge(c_ms, n + 1)
                    ps = banks.wait(dve, f"c{t}")
                    if n >= 2:
                        banks.wait(dve, f"cT{AB_ORDER[n - 2]}")
                    for g, name in enumerate(("mla_cq_gain_2", "mla_ckv_gain_2")):
                        ins = dve.scalar_tensor_tensor(cn[:, t % 2, RANK * g:RANK * g + RANK],
                                                       ps[:, RANK * g:RANK * g + RANK],
                                                       rstd[:, 16 + 2 * t + g:17 + 2 * t + g], gain[name],
                                                       ALU.mult, ALU.mult)
                    ins.then_inc(c_ready, 1)

            norm_rows(2, view(HIGH, 4, D))
            turn(2, hT, [(T, 512, 4)])
            latent_norms(AB_ORDER[0:2])
            def rope(dst, src, heads, table, t, tmp):
                f = table.shape[-1]
                n = heads * 2 * f
                parts = "p h (a s f) -> p h a s f"
                s5, d5 = src.rearrange(parts, a=2, s=2), dst.rearrange(parts, a=2, s=2)
                ts = [tmp[:, i * n:(i + 1) * n].rearrange("p (h a f) -> p h a f", h=heads, a=2) for i in range(4)]
                cos, sin = (outer(table[:, t, i], heads) for i in range(2))
                x1, x2 = s5[:, :, :, 0, :], s5[:, :, :, 1, :]
                dve.tensor_tensor(ts[0], x1, cos, ALU.mult)
                dve.tensor_tensor(ts[1], x2, sin, ALU.mult)
                dve.tensor_tensor(ts[2], x2, cos, ALU.mult)
                link(dve.tensor_tensor(ts[3], x1, sin, ALU.mult))
                dve.tensor_tensor(d5[:, :, :, 0, :], ts[0], ts[1], ALU.subtract)
                return dve.tensor_tensor(d5[:, :, :, 1, :], ts[2], ts[3], ALU.add)

            def squares(src, tmp, o, heads, d):
                tv = tmp[:, 0:heads * d].rearrange("p (h d) -> p h d", h=heads)
                link(dve.tensor_tensor(tv, src, src, ALU.mult))
                return dve.tensor_reduce(sums[:, o:o + heads], tv, AX.X, ALU.add)

            def grouped_norms(n, q, k, qn, kn, t, base):
                ta, tb, tr = view(base, 512), view(base + 512, 512), view(base + 1024, 1024)
                done = n if n < 8 else n - 4
                if done not in (0, 4):
                    dve.wait_ge(gqk_ready, done)
                if q is not None:
                    squares(q, ta, 32, GH, GD)
                nq = GH if q is not None else 0
                squares(k, tb, 32 + nq, KVH, GD).then_inc(qk_ms, 1)
                dve.wait_ge(qk_rstd, n + 1)
                if q is not None:
                    tv = ta.rearrange("p (g v d) -> p v g d", g=GPK, v=KVH)
                    link(dve.tensor_tensor(tv, q.rearrange("p (v g) d -> p v g d", v=KVH),
                                           inner(rstd[:, 32:32 + GH].rearrange("p (v g) -> p v g", v=KVH), GD), ALU.mult))
                    tn = ta.rearrange("p (h d) -> p h d", h=GH)
                    link(dve.tensor_tensor(tn if t < TT else q, tn, outer(gain[qn], GH), ALU.mult))
                    if t < TT:
                        link(rope(q, tn, GH, rope_gqa, t, tr))
                tk = tb[:, 0:KVH * GD].rearrange("p (h d) -> p h d", h=KVH)
                link(dve.tensor_tensor(tk, k, inner(rstd[:, 32 + nq:32 + nq + KVH], GD), ALU.mult))
                if t < TT:
                    link(dve.tensor_tensor(tk, tk, outer(gain[kn], KVH), ALU.mult))
                    ins = rope(k, tk, KVH, rope_gqa, t, tr)
                else:
                    ins = dve.tensor_tensor(k, tk, outer(gain[kn], KVH), ALU.mult)
                ins.then_inc(gqk_ready, 1)

            def ab_grouped(n):
                t = AB_ORDER[n]
                dve.wait_ge(pj_ready, n + 1)
                grouped_norms(n, pj[:, t, 32:544].rearrange("p (h d) -> p h d", h=GH),
                              pj[:, t, 544:672].rearrange("p (h d) -> p h d", h=KVH), "gqa_q_gain_2", "gqa_k_gain_2", t,
                              HIGH + 1024)

            for n in range(2):
                ab_grouped(n)
            dve.wait_ge(gathered_y, 16 * 4)
            dve.wait_ge(gate_bc, 4)
            for t in range(TT):
                ya, yb = y_tok[:, t, 0, :], y_tok[:, t, 1, :]
                link(dve.tensor_scalar(ya, ya, gates_ab[:, t, 0:1], None, ALU.mult))
                link(dve.scalar_tensor_tensor(ya, yb, gates_ab[:, t, 1:2], ya, ALU.mult, ALU.add))
                link(dve.tensor_tensor(ya, ya, gate_rows[:, 1, :], ALU.mult))
                dve.tensor_tensor(X[:, t, :], X[:, t, :], ya, ALU.add).then_inc(x_moe, 1)
            dve.wait_ge(rstd_ready, 4)
            dve.wait_ge(final_in, 16)
            for t in range(TT):
                dve.scalar_tensor_tensor(X[:, t, :], X[:, t, :], rstd[:, t:t + 1], final_row, ALU.mult, ALU.mult)\
                   .then_inc(block1_done, 1)
            dve.wait_ge(block1_done, 2)
            banks.wait(dve, f"cT{AB_ORDER[1]}")
            norm_rows(4, view(HIGH, 4, D))
            turn(3, hT, [(0, T, 3)])
            latent_norms(AB_ORDER[2:4])

            for n in range(2, 4):
                ab_grouped(n)
            for n, t in enumerate(AB_ORDER):
                q, k = q_t[n % 2], k_t[n % 2]
                dve.wait_ge(qa_copied, 2 * n + 2)
                dve.wait_ge(kv_copied, 2 * n + 2)
                if n >= 2:
                    banks.wait(dve, f"qkT{AB_ORDER[n - 2]}11")
                if n >= 1:
                    dve.wait_ge(qk_ready, n)
                dve.tensor_copy(k[:, :, NOPE:MD], outer(pj[:, t, 0:ROT], MH))
                link(squares(q, tmp1, 0, MH, MD))
                squares(k, tmp1, MH, MH, MD).then_inc(qk_ms, 1)
                dve.wait_ge(qk_rstd, 4 + n + 1)
                for src, o, gn in ((q, 0, "mla_q_gain_2"), (k, MH, "mla_k_gain_2")):
                    link(dve.tensor_tensor(src, src, inner(rstd[:, o:o + MH], MD), ALU.mult))
                    ins = dve.tensor_tensor(src, src, outer(gain[gn], MH), ALU.mult)
                    if t < TT:
                        link(ins)
                        ins = rope(src[:, :, NOPE:MD], src[:, :, NOPE:MD], MH, rope_mla, t, tmp1)
                        if o == 0:
                            link(ins)
                ins.then_inc(qk_ready, 1)

            def attention(units, base, nkeys, dst, between, sink):
                def peak(n):
                    u = base + n
                    t, h = units[n][2], units[n][1]
                    ps = banks.wait(dve, f"s{u}")
                    nm = small[:, 512 + u % 4:513 + u % 4]
                    if not sink:
                        dve.tensor_reduce(nm, ps[:, 0:nkeys(n)], AX.X, ALU.max, negate=True).then_inc(s_max, 1)
                        return
                    w = ps[:, P * (1 - t):P * (2 - t)]
                    m = small[:, 516 + u % 4:517 + u % 4]
                    link(dve.tensor_tensor(w, w, window[:, t, :], ALU.add))
                    link(dve.tensor_reduce(m, ps[:, 0:nkeys(n)], AX.X, ALU.max))
                    dve.tensor_scalar(nm, m, gain["win_sink_2"][:, h:h + 1], -1.0, ALU.max, ALU.mult).then_inc(s_max, 1)

                def turned(n):
                    u = base + n
                    if u % 2 == 1:
                        ps = banks.wait(dve, f"p{u}")
                        if n >= 3:
                            banks.wait(dve, f"av{u - 3}")
                        dve.tensor_copy(probT[u % 3][:, 0:nkeys(n)], ps[:, 0:nkeys(n)]).then_inc(pT_v, 1)

                def mix(n):
                    u = base + n
                    ps = banks.wait(dve, f"av{u}")
                    den, rden = small[:, 520 + u % 4:521 + u % 4], small[:, 524 + u % 4:525 + u % 4]
                    dve.wait_ge(s_exp, u + 1)
                    if sink:
                        link(dve.tensor_tensor(den, den, small[:, 528 + u % 4:529 + u % 4], ALU.add))
                    link(dve.reciprocal(rden, den))
                    d = dst(units[n])
                    dve.scalar_tensor_tensor(d, ps[:, 0:64], rden, d, ALU.mult, ALU.mult).then_inc(mixed, 1)

                peak(0)
                for n in range(len(units)):
                    if n + 1 < len(units):
                        peak(n + 1)
                    turned(n)
                    if n >= 1:
                        mix(n - 1)
                    between(n)
                mix(len(units) - 1)

            def ab_between(n):
                if n % 8 == 4 and 1 <= n // 8 < 6:
                    mod_col(18 + n // 8 - 1)
                if n == 61:
                    mod_col(23)

            dve.wait_ge(gate4_ready, 4)
            attention(AB_UNITS, 0, lambda n: 512 if AB_UNITS[n][2] < TT else 256,
                      lambda u: gates4[:, u[2], (0 if u[0] == "m" else 512) + 64 * u[1]:(64 if u[0] == "m" else 576) + 64 * u[1]],
                      ab_between, False)
            dve.wait_ge(modcol_ready, 24)
            gate(2, mod2[:, 0, 16:24, 0])
            gate(3, mod2[:, 0, 16:24, 1])
            for m in range(2):
                coefficients(5 + m, mod2[:, 1, 8:16, m], mod2[:, 1, 0:8, m], None)
            dve.wait_ge(gate_bc, 8)
            for c in range(2):
                for t in range(4):
                    add_gated(f"aby{c}{t}", view(HIGH, 512), 2 if t < TT else 3, c, t)
            norm_rows(5, view(HIGH, 4, D))
            turn(4, hT, [(0, T, 5), (T, 512, 6)])
            for t in range(4):
                if t < TT:
                    dve.wait_ge(cdq_ready, t + 1)
                dve.wait_ge(cdkv_ready, t + 1)
                grouped_norms(8 + t, cq_sb[:, t, :].rearrange("p (h d) -> p h d", h=GH) if t < TT else None,
                              ckv_sb[:, t, 0:P].rearrange("p (h d) -> p h d", h=KVH), "win_q_gain_2", "win_k_gain_2", t,
                              HIGH + 7168)
            dve.wait_ge(cdT_ready, 8)
            for o in (0, T + 1):
                link(dve.memset(u_pad[:, :, o:o + 1], 0.0))
            link(dve.tensor_tensor(u_pad[:, :, 1:T + 1], gcT, ghT, ALU.mult))
            taps = column("conv_w_2")
            for k in range(TAPS):
                for c in range(4):
                    w = taps[:, 4 * k + c:4 * k + c + 1]
                    if k == 0:
                        ins = dve.tensor_scalar(conv[:, c, :], u_pad[:, c, 0:T], w, None, ALU.mult)
                    else:
                        ins = dve.scalar_tensor_tensor(conv[:, c, :], u_pad[:, c, k:k + T], w, conv[:, c, :],
                                                       ALU.mult, ALU.add)
                link(ins)
            link(dve.tensor_tensor(conv, conv, gbT, ALU.mult))
            dve.tensor_tensor(mixT2[:, 4:8, :], conv, gaT, ALU.mult).then_inc(cd_conv, 1)
            dve.wait_ge(cdg_ready, 2)
            attention(CD_UNITS, NU, lambda n: 512, lambda u: ga_sb[:, u[2], 64 * u[1]:64 * u[1] + 64], lambda n: None, True)
            gate(4, mod2[:, 1, 16:24, 0])
            dve.wait_ge(gate_bc, 10)
            for c in range(2):
                for t in range(TT):
                    add_gated(f"cdy{c}{t}", ctmp1, 4, c, t)

        @block.gpsimd
        def _(pool):
            pool.memset(silu_c[:, :, :, :].rearrange("p b k m -> p (b k m)"), 0.0).then_inc(silu_zeroed, 1)
            for n, w in gain_widths:
                src = a[n]
                nd = len(src.shape)
                names = "abcd"[:nd]
                flat = src.rearrange("%s -> (%s)" % (" ".join(names), " ".join(names))) if nd > 1 else src
                pool.dma_start(gain[n], flat.partition_broadcast(P)).then_inc(gains_in, 16)
            pool.memset(gate_rows[:, :, :], 0.0).then_inc(gate_rows_zero, 1)
            pool.wait_ge(gate_rows_zero, 1)
            pool.wait_ge(q_ready, 2)
            for e in range(NE):
                pool.dma_start(y_rows[e * T + CAP:(e + 1) * T, :].rearrange("(p j) d -> p j d", j=2),
                               gate_rows[0:(T - CAP) // 2, :, :]).then_inc(rows_zeroed, 16)
            pool.wait_ge(xn_ready, 4)
            pool.dma_start(X[:, 2:4, :], a["ctx_2"][0].rearrange("(t p) d -> p t d", p=P)).then_inc(ctx2_in, 16)
            pool.wait_ge(hg_a, 8)
            pool.wait_ge(hg_v, 8)

            def stage(e, b):
                pool.tensor_copy(hs[b], hg[:, :, bass.ds(e * CAP, CAP)]).then_inc(hs_ready, 1)

            stage(0, 0)
            stage(1, 1)
            with pool.Fori(1, NE // 2) as i:
                for b in range(2):
                    e = i * 2 + b
                    pool.wait_ge(up_done, e - 1)
                    stage(e, b)
            for b in range(2):
                pool.wait_ge(stored[b], 32 * (NE // 2 + 1))
            pool.wait_ge(x_stored, 32 * (NE * EXTRA + 1))
            pool.dma_start(final_row, a["final_g"].partition_broadcast(P)).then_inc(final_in, 16)
            for t in range(TT):
                for j in range(2):
                    pool.indirect_dma_start(out=y_tok[:, t, j, :], out_offset=None, in_=y_rows[:, :],
                                            in_offset=bass.IndirectOffsetOnAxis(ap=route_idx[:, t, j:j + 1], axis=0))\
                        .then_inc(gathered_y, 16)


_INS = ["x", "c", "ctx", "c_ctx", "norm1_g", "norm2_g", "w_mod", "b_mod", "gla_w_in", "gla_w_gate_a", "gla_w_gate_b",
        "gla_b_gate", "gla_norm_g", "gla_w_out", "w_router", "b_router", "w_gate_e", "w_up_e", "w_down_e", "final_g",
        "c_2", "ctx_2", "c_ctx_2", "mod_w_2", "mod_b_2", "ab_w_in_2", "ab_w_out_2", "mla_cq_gain_2", "mla_ckv_gain_2",
        "mla_w_uq_2", "mla_w_ukv_2", "mla_q_gain_2", "mla_k_gain_2", "gqa_q_gain_2", "gqa_k_gain_2", "cd_w_in_2",
        "cd_w_out_2", "win_q_gain_2", "win_k_gain_2", "win_sink_2", "conv_w_2"]


def kernel(**inputs):
    import numpy as _np
    import concourse.bacc as _bacc
    from concourse import mybir as _mybir
    from concourse.bass_utils import run_bass_kernel_spmd as _run

    nc = _bacc.Bacc("TRN2", target_bir_lowering=False, num_devices=1)
    arrays, args = {}, {}
    for name in _INS + ["constants"]:
        arr = constant_table() if name == "constants" else _np.ascontiguousarray(inputs[name])
        arrays[f"in_{name}_dram"] = arr
        args[name] = nc.dram_tensor(f"in_{name}_dram", arr.shape, _mybir.dt.from_np(arr.dtype), kind="ExternalInput").ap()
    out = nc.dram_tensor("out_0_dram", (1, T, D), F32, kind="ExternalOutput").ap()
    build(nc, args, out)
    r = _run(nc, [arrays], core_ids=[0])
    return r.results[0]["out_0_dram"]
```
